# Optimizing a Trainium2 kernel written in Bass

```python
import math
import jax, jax.numpy as jnp
from jax import lax
import numpy as np

D_MODEL = 1024
BATCH = 1
SEQ = 1024
DEPTH = 1

GDN_HEADS = 4
GDN_HEAD_DIM = 128
GDN_WIDTH = GDN_HEADS * GDN_HEAD_DIM
GDN_CONV = 4
GDN_CHUNK = 64
DIL_HEADS = 8
DIL_HEAD_DIM = 64
DIL_WIDTH = DIL_HEADS * DIL_HEAD_DIM
DIL_PATTERNS = ((128, 1), (512, 4), (2048, 16))
BAND_BLOCK = 128
MIX_WIDTH = GDN_WIDTH + DIL_WIDTH
IN_COLS = 3 * GDN_WIDTH + GDN_WIDTH + 2 * GDN_HEADS + 3 * DIL_WIDTH
D_FF = 2816
FFN_CONV = 3
EPS = 1e-6


def rmsnorm(x, w):
    xf = x.astype(jnp.float32)
    y = xf * lax.rsqrt(jnp.mean(xf * xf, axis=-1, keepdims=True) + EPS)
    return (y * w.astype(jnp.float32)).astype(x.dtype)

def l2norm(x):
    return x * lax.rsqrt(jnp.sum(x * x, axis=-1, keepdims=True) + EPS)

def causal_dwconv(x, w):
    K = w.shape[0]
    S = x.shape[1]
    xp = jnp.pad(x, ((0, 0), (K - 1, 0), (0, 0)))
    out = xp[:, 0:S, :] * w[0]
    for i in range(1, K):
        out = out + xp[:, i:i + S, :] * w[i]
    return out

def gated_delta_rule(q, k, v, g, beta):
    B, S, H, Dk = q.shape
    Dv = v.shape[-1]
    C = GDN_CHUNK
    nc = S // C

    def chunk_vec(t):
        return t.reshape(B, nc, C, H, t.shape[-1]).transpose(1, 0, 3, 2, 4)

    def chunk_sc(t):
        return t.reshape(B, nc, C, H).transpose(1, 0, 3, 2)

    qc, kc, vc = chunk_vec(q), chunk_vec(k), chunk_vec(v)
    bc = chunk_sc(beta)
    gc = jnp.cumsum(chunk_sc(g), axis=-1)
    idx = jnp.arange(C)
    incl = idx[:, None] >= idx[None, :]
    strict = idx[:, None] > idx[None, :]
    diff = gc[..., :, None] - gc[..., None, :]
    dec_incl = jnp.where(incl, jnp.exp(jnp.where(incl, diff, 0.0)), 0.0)
    dec_strict = jnp.where(strict, dec_incl, 0.0)
    kk = jnp.einsum('nbhtd,nbhjd->nbhtj', kc, kc)
    lmat = dec_strict * kk * bc[..., None, :]
    gam = jnp.exp(gc)[..., None]
    rhs = jnp.concatenate([vc, gam * kc], axis=-1)
    sol = lax.linalg.triangular_solve(lmat, rhs, left_side=True, lower=True, unit_diagonal=True)
    u_v, w_k = sol[..., :Dv], sol[..., Dv:]
    attn = dec_incl * jnp.einsum('nbhtd,nbhjd->nbhtj', qc, kc) * bc[..., None, :]
    q_dec = gam * qc
    k_end = kc * (jnp.exp(gc[..., -1:] - gc) * bc)[..., None]
    g_end = jnp.exp(gc[..., -1])

    def step(state, xs):
        uv, wk, qd, at, ke, ge = xs
        u = uv - jnp.einsum('bhck,bhkv->bhcv', wk, state)
        o = jnp.einsum('bhck,bhkv->bhcv', qd, state) + jnp.einsum('bhcj,bhjv->bhcv', at, u)
        state = ge[..., None, None] * state + jnp.einsum('bhck,bhcv->bhkv', ke, u)
        return state, o

    s0 = jnp.zeros((B, H, Dk, Dv), jnp.float32)
    _, o = lax.scan(step, s0, (u_v, w_k, q_dec, attn, k_end, g_end))
    return o.transpose(1, 0, 3, 2, 4).reshape(B, S, H, Dv)

def band_attention(q, k, v, n_back):
    L, Dh = q.shape[-2], q.shape[-1]
    nb = -(-L // BAND_BLOCK)
    pad = nb * BAND_BLOCK - L
    padcfg = [(0, 0)] * (q.ndim - 2) + [(0, pad), (0, 0)]
    lead = q.shape[:-2]

    def blocks(t):
        return jnp.pad(t, padcfg).reshape(*lead, nb, BAND_BLOCK, Dh)

    qb, kb, vb = blocks(q), blocks(k), blocks(v)

    def with_prev(t):
        prev = jnp.concatenate([jnp.zeros_like(t[..., :1, :, :]), t[..., :-1, :, :]], axis=-3)
        return jnp.concatenate([prev, t], axis=-2)

    kk, vv = with_prev(kb), with_prev(vb)
    s = jnp.einsum('...nqd,...nkd->...nqk', qb, kk)
    blk = jnp.arange(nb)[:, None, None] * BAND_BLOCK
    qpos = blk + jnp.arange(BAND_BLOCK)[None, :, None]
    kpos = blk - BAND_BLOCK + jnp.arange(2 * BAND_BLOCK)[None, None, :]
    dist = qpos - kpos
    valid = (dist >= 0) & (dist <= n_back) & (kpos >= 0)
    s = jnp.where(valid, s, -jnp.inf)
    m = jnp.max(s, axis=-1)
    p = jnp.exp(s - m[..., None])
    den = jnp.sum(p, axis=-1)
    num = jnp.einsum('...nqk,...nkd->...nqd', p, vv)
    num = num.reshape(*lead, nb * BAND_BLOCK, Dh)[..., :L, :]
    den = den.reshape(*lead, nb * BAND_BLOCK)[..., :L]
    m = m.reshape(*lead, nb * BAND_BLOCK)[..., :L]
    return num, den, m

def dilated_attention(q, k, v):
    B, S, H, Dh = q.shape
    qf = q.astype(jnp.float32).transpose(0, 2, 1, 3) * (Dh ** -0.5)
    kf = k.astype(jnp.float32).transpose(0, 2, 1, 3)
    vf = v.astype(jnp.float32).transpose(0, 2, 1, 3)
    nums, dens, ms = [], [], []
    for window, dil in DIL_PATTERNS:
        L = S // dil

        def stride(t):
            return t.reshape(B, H, L, dil, Dh).transpose(0, 1, 3, 2, 4)

        num, den, m = band_attention(stride(qf), stride(kf), stride(vf), window // dil)
        nums.append(num.transpose(0, 1, 3, 2, 4).reshape(B, H, S, Dh))
        dens.append(den.transpose(0, 1, 3, 2).reshape(B, H, S))
        ms.append(m.transpose(0, 1, 3, 2).reshape(B, H, S))
    m_all = jnp.maximum(jnp.maximum(ms[0], ms[1]), ms[2])
    wts = [jnp.exp(mi - m_all) for mi in ms]
    num_tot = wts[0][..., None] * nums[0] + wts[1][..., None] * nums[1] + wts[2][..., None] * nums[2]
    den_tot = wts[0] * dens[0] + wts[1] * dens[1] + wts[2] * dens[2]
    out = num_tot / den_tot[..., None]
    return out.transpose(0, 2, 1, 3).reshape(B, S, H * Dh)

def hybrid_layer(x, norm1_w, w_in, conv_qkv_w, a_log, dt_bias, gdn_norm_w, w_out,
                 norm2_w, w_up, ffn_conv_w, w_down):
    B, S, _ = x.shape
    h = rmsnorm(x, norm1_w)
    proj = h @ w_in
    o1 = 3 * GDN_WIDTH
    o2 = o1 + GDN_WIDTH
    o3 = o2 + GDN_HEADS
    o4 = o3 + GDN_HEADS
    qkv_a, z_a, b_a, a_a, qkv_b = (proj[..., :o1], proj[..., o1:o2], proj[..., o2:o3],
                                   proj[..., o3:o4], proj[..., o4:])
    qkv_a = jax.nn.silu(causal_dwconv(qkv_a, conv_qkv_w)).astype(jnp.float32)
    qa = qkv_a[..., :GDN_WIDTH].reshape(B, S, GDN_HEADS, GDN_HEAD_DIM)
    ka = qkv_a[..., GDN_WIDTH:2 * GDN_WIDTH].reshape(B, S, GDN_HEADS, GDN_HEAD_DIM)
    va = qkv_a[..., 2 * GDN_WIDTH:].reshape(B, S, GDN_HEADS, GDN_HEAD_DIM)
    qa = l2norm(qa) * (GDN_HEAD_DIM ** -0.5)
    ka = l2norm(ka)
    beta = jax.nn.sigmoid(b_a.astype(jnp.float32))
    g = -jnp.exp(a_log.astype(jnp.float32)) * jax.nn.softplus(
        a_a.astype(jnp.float32) + dt_bias.astype(jnp.float32))
    o_a = gated_delta_rule(qa, ka, va, g, beta)
    z = z_a.astype(jnp.float32).reshape(B, S, GDN_HEADS, GDN_HEAD_DIM)
    o_a = (rmsnorm(o_a, gdn_norm_w) * jax.nn.silu(z)).reshape(B, S, GDN_WIDTH).astype(x.dtype)
    qb = qkv_b[..., :DIL_WIDTH].reshape(B, S, DIL_HEADS, DIL_HEAD_DIM)
    kb = qkv_b[..., DIL_WIDTH:2 * DIL_WIDTH].reshape(B, S, DIL_HEADS, DIL_HEAD_DIM)
    vb = qkv_b[..., 2 * DIL_WIDTH:].reshape(B, S, DIL_HEADS, DIL_HEAD_DIM)
    o_b = dilated_attention(qb, kb, vb).astype(x.dtype)
    x = x + jnp.concatenate([o_a, o_b], axis=-1) @ w_out
    h = rmsnorm(x, norm2_w)
    u = causal_dwconv(h @ w_up, ffn_conv_w)
    gate, up = u[..., :D_FF], u[..., D_FF:]
    x = x + (jax.nn.silu(gate) * up) @ w_down
    return x

def first_inputs(seed: int = 0) -> dict:
    key = jax.random.key(seed)
    ks = jax.random.split(key, 14)
    f32 = jnp.float32
    x = jax.random.normal(ks[0], (BATCH, SEQ, D_MODEL), f32)
    norm1_w = 1.0 + 0.02 * jax.random.normal(ks[1], (DEPTH, D_MODEL), f32)
    w_in = jax.random.normal(ks[2], (DEPTH, D_MODEL, IN_COLS), f32) * D_MODEL ** -0.5
    conv_qkv_w = jax.random.normal(ks[3], (DEPTH, GDN_CONV, 3 * GDN_WIDTH), f32) * GDN_CONV ** -0.5
    a_log = jnp.log(jax.random.uniform(ks[4], (DEPTH, GDN_HEADS), f32, 1.0, 16.0))
    dt = jnp.exp(jax.random.uniform(ks[5], (DEPTH, GDN_HEADS), f32, math.log(1e-3), math.log(1e-1)))
    dt_bias = dt + jnp.log(-jnp.expm1(-dt))
    gdn_norm_w = 1.0 + 0.02 * jax.random.normal(ks[6], (DEPTH, GDN_HEAD_DIM), f32)
    w_out = jax.random.normal(ks[7], (DEPTH, MIX_WIDTH, D_MODEL), f32) * MIX_WIDTH ** -0.5
    norm2_w = 1.0 + 0.02 * jax.random.normal(ks[8], (DEPTH, D_MODEL), f32)
    w_up = jax.random.normal(ks[9], (DEPTH, D_MODEL, 2 * D_FF), f32) * D_MODEL ** -0.5
    ffn_conv_w = jax.random.normal(ks[10], (DEPTH, FFN_CONV, 2 * D_FF), f32) * FFN_CONV ** -0.5
    w_down = jax.random.normal(ks[11], (DEPTH, D_FF, D_MODEL), f32) * D_FF ** -0.5
    final_norm_w = 1.0 + 0.02 * jax.random.normal(ks[12], (D_MODEL,), f32)
    return {"x": x, "norm1_w": norm1_w, "w_in": w_in, "conv_qkv_w": conv_qkv_w,
            "a_log": a_log, "dt_bias": dt_bias, "gdn_norm_w": gdn_norm_w, "w_out": w_out,
            "norm2_w": norm2_w, "w_up": w_up, "ffn_conv_w": ffn_conv_w, "w_down": w_down,
            "final_norm_w": final_norm_w}

def first_block(x, norm1_w, w_in, conv_qkv_w, a_log, dt_bias, gdn_norm_w, w_out,
              norm2_w, w_up, ffn_conv_w, w_down, final_norm_w):
    for l in range(DEPTH):
        x = hybrid_layer(x, norm1_w[l], w_in[l], conv_qkv_w[l], a_log[l], dt_bias[l],
                         gdn_norm_w[l], w_out[l], norm2_w[l], w_up[l], ffn_conv_w[l], w_down[l])
    return rmsnorm(x, final_norm_w)


D_MIX = D_MODEL
D_A = D_MIX // 2
D_B = D_MIX - D_A
CHUNK = 128
H_A = 4
HD_A = D_A // H_A
H_B = 4
HD_B = D_B // H_B
CONV_W = 31
D_FF_2 = 4 * D_MODEL
IN_COLS_2 = 2 * D_A + 2 * D_B


def rms_norm(x, g):
    xf = x.astype(jnp.float32)
    y = xf * lax.rsqrt(jnp.mean(xf * xf, axis=-1, keepdims=True) + EPS)
    return (y * g.astype(jnp.float32)).astype(x.dtype)

def layer_norm(x, g, b):
    xf = x.astype(jnp.float32)
    mu = jnp.mean(xf, axis=-1, keepdims=True)
    var = jnp.mean(jnp.square(xf - mu), axis=-1, keepdims=True)
    y = (xf - mu) * lax.rsqrt(var + EPS)
    return (y * g.astype(jnp.float32) + b.astype(jnp.float32)).astype(x.dtype)

def spatial_gating(u_a, v_a, ln_g, ln_b, w_s, b_s):
    bsz, seq, _ = u_a.shape
    u = jax.nn.gelu(u_a, approximate=False)
    v = layer_norm(jax.nn.gelu(v_a, approximate=False), ln_g, ln_b)
    v = v.reshape(bsz, seq // CHUNK, CHUNK, H_A, HD_A)
    mask = jnp.tril(jnp.ones((CHUNK, CHUNK), dtype=w_s.dtype))
    w = w_s * mask[None]
    mixed = jnp.einsum('hts,bcshd->bcthd', w, v)
    mixed = mixed + jnp.transpose(b_s)[None, None, :, :, None]
    return u * mixed.reshape(bsz, seq, D_A)

def conformer_conv(val_b, gate_b, conv_w, conv_b, ln_g, ln_b):
    bsz, seq, _ = val_b.shape
    g = val_b * jax.nn.sigmoid(gate_b)
    c = lax.conv_general_dilated(
        g, conv_w[:, None, :].astype(g.dtype),
        window_strides=(1,), padding=[(CONV_W - 1, 0)],
        dimension_numbers=('NWC', 'WIO', 'NWC'),
        feature_group_count=D_B)
    c = c + conv_b
    c = layer_norm(c.reshape(bsz, seq, H_B, HD_B),
                   ln_g.reshape(H_B, HD_B), ln_b.reshape(H_B, HD_B))
    return jax.nn.silu(c).reshape(bsz, seq, D_B)

def second_inputs(seed: int = 0) -> dict:
    key = jax.random.key(seed)
    ks = jax.random.split(key, 20)
    f32 = jnp.float32
    nrm = lambda k, shape, scale: jax.random.normal(k, shape, f32) * scale
    return {
        "x": jax.random.normal(ks[0], (BATCH, SEQ, D_MODEL), f32),
        "norm1_g": 1.0 + nrm(ks[1], (DEPTH, D_MODEL), 0.05),
        "w_in": nrm(ks[2], (DEPTH, D_MODEL, IN_COLS_2), D_MODEL ** -0.5),
        "sgu_ln_g": 1.0 + nrm(ks[3], (DEPTH, D_A), 0.05),
        "sgu_ln_b": nrm(ks[4], (DEPTH, D_A), 0.02),
        "sgu_w": nrm(ks[5], (DEPTH, H_A, CHUNK, CHUNK), CHUNK ** -0.5),
        "sgu_b": 1.0 + nrm(ks[6], (DEPTH, H_A, CHUNK), 0.1),
        "conv_w": nrm(ks[7], (DEPTH, CONV_W, D_B), CONV_W ** -0.5),
        "conv_b": nrm(ks[8], (DEPTH, D_B), 0.02),
        "conv_ln_g": 1.0 + nrm(ks[9], (DEPTH, D_B), 0.05),
        "conv_ln_b": nrm(ks[10], (DEPTH, D_B), 0.02),
        "w_out": nrm(ks[11], (DEPTH, D_MIX, D_MODEL), D_MIX ** -0.5),
        "norm2_g": 1.0 + nrm(ks[12], (DEPTH, D_MODEL), 0.05),
        "w_ff1": nrm(ks[13], (DEPTH, D_MODEL, D_FF_2), D_MODEL ** -0.5),
        "w_ff2": nrm(ks[14], (DEPTH, D_FF_2, D_MODEL), D_FF_2 ** -0.5),
        "final_g": 1.0 + nrm(ks[15], (D_MODEL,), 0.05),
    }

def second_block(x, norm1_g, w_in, sgu_ln_g, sgu_ln_b, sgu_w, sgu_b, conv_w, conv_b,
              conv_ln_g, conv_ln_b, w_out, norm2_g, w_ff1, w_ff2, final_g):
    for l in range(DEPTH):
        h = rms_norm(x, norm1_g[l])
        proj = jnp.einsum('bsd,dc->bsc', h, w_in[l])
        u_a = proj[..., :D_A]
        v_a = proj[..., D_A:2 * D_A]
        val_b = proj[..., 2 * D_A:2 * D_A + D_B]
        gate_b = proj[..., 2 * D_A + D_B:]
        a_out = spatial_gating(u_a, v_a, sgu_ln_g[l], sgu_ln_b[l], sgu_w[l], sgu_b[l])
        b_out = conformer_conv(val_b, gate_b, conv_w[l], conv_b[l],
                               conv_ln_g[l], conv_ln_b[l])
        mix = jnp.concatenate([a_out, b_out], axis=-1)
        x = x + jnp.einsum('bsc,cd->bsd', mix, w_out[l])
        h = rms_norm(x, norm2_g[l])
        f = jnp.square(jax.nn.relu(jnp.einsum('bsd,df->bsf', h, w_ff1[l])))
        x = x + jnp.einsum('bsf,fd->bsd', f, w_ff2[l])
    return rms_norm(x, final_g)


def setup_inputs(seed=0):
    out = dict(first_inputs(seed))
    for name, value in second_inputs(seed + 1).items():
        if name != "x":
            out[name + "_2"] = value
    return out


def reference(
    x, norm1_w, w_in, conv_qkv_w, a_log, dt_bias, gdn_norm_w, w_out, norm2_w, w_up, ffn_conv_w,
    w_down, final_norm_w, norm1_g_2, w_in_2, sgu_ln_g_2, sgu_ln_b_2, sgu_w_2, sgu_b_2, conv_w_2,
    conv_b_2, conv_ln_g_2, conv_ln_b_2, w_out_2, norm2_g_2, w_ff1_2, w_ff2_2, final_g_2,
):
    x = first_block(
        x, norm1_w, w_in, conv_qkv_w, a_log, dt_bias, gdn_norm_w, w_out, norm2_w, w_up,
        ffn_conv_w, w_down, final_norm_w,
    )
    return second_block(
        x, norm1_g_2, w_in_2, sgu_ln_g_2, sgu_ln_b_2, sgu_w_2, sgu_b_2, conv_w_2, conv_b_2,
        conv_ln_g_2, conv_ln_b_2, w_out_2, norm2_g_2, w_ff1_2, w_ff2_2, final_g_2,
    )


_drawn_inputs = setup_inputs


def setup_inputs(seed=0):
    import zlib

    import numpy as np

    out = dict(_drawn_inputs(seed))
    spreads = {}
    factors = {'norm1_w': 3.159,
     'gdn_norm_w': 5.619,
     'norm2_w': 3.696,
     'sgu_ln_g_2': 4.012,
     'sgu_ln_b_2': 8.0,
     'conv_b_2': 3.793,
     'conv_ln_g_2': 2.751,
     'conv_ln_b_2': 7.267}
    for name, (base, spread) in spreads.items():
        noise = np.random.default_rng([zlib.crc32(name.encode()), seed]).standard_normal(out[name].shape)
        drawn = base * np.exp(spread * noise) if base else spread * noise
        out[name] = __import__('jax').numpy.asarray(drawn.astype(out[name].dtype))
    for name, factor in factors.items():
        out[name] = (out[name] * factor).astype(out[name].dtype)
    return out
```

```python
from contextlib import ExitStack

import numpy as np

import concourse.bass as bass
from concourse import mybir

F32 = mybir.dt.float32
F32R = mybir.dt.float32r
ACT = mybir.ActivationFunctionType
ALU = mybir.AluOpType
AX_X = mybir.AxisListType.X

P = 128
D = 1024
S = 1024
KT = D // P
TT = S // P
HALF = 512
EPS = 1e-6
GH = 4
AH = 8
FF1 = 2816 // P
FF2 = 4096 // P
LEVELS = 7
TAPS31 = 31

U_QKVB, U_QKV, U_Z, U_OUT1 = 0, 12, 24, 28
U_FFN1 = U_OUT1 + KT
U_IN2 = U_FFN1 + 3 * FF1
U_OUT2 = U_IN2 + 16
U_FFN2 = U_OUT2 + KT
U_END = U_FFN2 + 2 * FF2
X_OUT1 = KT
X_FFN1 = X_OUT1 + KT
X_MID = X_FFN1 + KT * FF1
X_OUT2 = X_MID + KT
X_FFN2 = X_OUT2 + KT
X_END = X_FFN2 + KT * FF2
C_N1, C_N2, C_NF, C_M1, C_M2, C_MF, C_CONV, C_CB, C_LG, C_LB = 0, 8, 16, 24, 32, 40, 48, 96, 100, 104
C_GN, C_FF01, C_FF2, C_C31 = 108, 128, 256, 384
T_RQ, T_RK, T_BETA, T_G, T_NGC, T_N = 0, 4, 8, 12, 16, 20


def first(ap, n):
    return ap.unsqueeze(2).broadcast_to([ap.shape[0], ap.shape[1], n])


def again(ap, n):
    return ap.unsqueeze(1).broadcast_to([ap.shape[0], n, ap.shape[1]])


def program(nc, a, out):
    ctx = ExitStack()
    with ctx:
        def dram(name, shape):
            return nc.dram_tensor(name, shape, F32, kind="Internal").ap()

        x_s, qkvz_s, qkvb_s = dram("x_s", [P, KT, S]), dram("qkvz_s", [P, 16, S]), dram("qkvb_s", [P, 12, S])

        def sb(name, shape, dt=F32, where=ctx):
            return where.enter_context(nc.sbuf_tensor(name, shape, dt))

        def sem(name):
            return ctx.enter_context(nc.semaphore(name))

        PS = ctx.enter_context(nc.psum_tensor("PS", [P, 8, HALF], F32))

        def acc(s):
            return PS[:, 2 * s:2 * s + 2, :].rearrange("p a b -> p (a b)")

        def heads(bank):
            return PS[:, bank, :].rearrange("p (h t) -> p h t", h=4)

        par = sb("par", [P, 512])
        ident = sb("ident", [P, P])
        triu = sb("triu", [P, P])
        ones = sb("ones", [P, P])
        small = sb("small", [P, 256])
        bah, bal, baw = sb("bah", [P, 8, 8], F32R), sb("bal", [P, 8, 8], F32R), sb("baw", [P, 8, 8])
        raw = sb("raw", [P, 2, D])
        wh, wl = sb("wh", [P, 4, D], F32R), sb("wl", [P, 4, D], F32R)
        hh, hl = sb("hh", [P, KT, S], F32R), sb("hl", [P, KT, S], F32R)

        with ExitStack() as z:
            strip, lmask = sb("strip", [P, S], where=z), sb("lmask", [P, LEVELS + 1, P], where=z)
            tab = sb("tab", [P, TT, T_N], where=z)
            ch = sb("ch", [P, 2, 16, P], where=z)
            qkvb = sb("qkvb", [P, 3, S], where=z)
            vb = sb("vb", [P, TT, P], where=z)
            G = {n: sb(n, [P, GH, P], where=z) for n in
                 "bm E gam kn qn v knT qnT kd qd ke LT AT T TT U u St Sg oz".split()}
            G["og"] = G["u"]
            cc = sb("cc", [P, 2, T_N], where=z)
            oc = sb("oc", [P, 8, GH], where=z)
            sm = sb("sm", [P, 2, S], where=z)
            tmpt = sm[:, 0, 0:HALF].rearrange("p (a b) -> p a b", b=64)
            pt = sb("pt", [P, 2, HALF], where=z)
            ob = sb("ob", [P, TT, P], where=z)
            ac = sb("ac", [P, 4, 16], where=z)
        x = sb("x", [P, KT, S])
        with ExitStack() as z:
            xin = sb("xin", [P, TT, D], where=z)
            pack = sb("pack", [P, 4, P], where=z)
        with ExitStack() as z:
            st = sb("st", [P, 4, S], where=z)
            cacc = sb("cacc", [P, 2, S], where=z)
            sqb = sb("sqb", [P, S], where=z)
        with ExitStack() as z:
            wh2, wl2 = sb("wh2", [P, 2, D], F32R, where=z), sb("wl2", [P, 2, D], F32R, where=z)
            fh, fl = sb("fh", [P, 2, S], F32R, where=z), sb("fl", [P, 2, S], F32R, where=z)
            gc = sb("gc", [P, S], where=z)
            uc = sb("uc", [P, S], where=z)
            nacc, sqt = sb("nacc", [P, S], where=z), sb("sqt", [P, 2, S], where=z)
            diag = sb("diag", [P, TT, P], where=z)
            hf = sb("hf", [P, 2, S], where=z)
        with ExitStack() as z:
            cg = sb("cg", [P, 5, S], where=z)
            sgb = sb("sgb", [P, S], where=z)
            sgw = sb("sgw", [P, 2, GH, P], where=z)
            bsb = sb("bsb", [P, GH, P], where=z)
            lng, lnb = sb("lng", [P, HALF], where=z), sb("lnb", [P, HALF], where=z)
            vt = sb("vt", [P, TT, HALF], where=z)
            ub = sb("ub", [P, GH, S], where=z)

        def whs(slot):
            return (wh[:, slot] if slot < 4 else wh2[:, slot - 4])

        def wls(slot):
            return (wl[:, slot] if slot < 4 else wl2[:, slot - 4])

        names = """const_loaded rows_loaded pack_loaded par_mm par_ready consts_set xin_loaded xt_mm x_written x_spilled
            w_hi w_lo w_used n_sq n_acc n_cols n_v n_sd n_diag n_R n_x n_hi n_lo v_chain
            tap0 conv silu sq_init col_mm ba_loaded ba_hi ba_lo st_written phase_end
            tab_dve tab_act tab_mm mask_loaded cc_ready tri_ready gc_mm kq_mm d_raw gam_ready d_ready
            e_ready vt_mm vb_ready tt0_ready o_copied og_ready kqn_ready v_mm v_ready kqT_mm kqT_ready eb_ready gram_mm lat_ready
            kqd_ready ke_ready sg_ready l_mm u0_ready tt0_raw lev_l lev_u lev_v lev_w lev_t lev_tt
            ks_mm r_ready u_mm u_ready s_ready os_mm osq oss o_v o_sd o_r oz_ready on_ready ot_mm oh_ready
            ol_ready s_mm s_max s_neg s_exp p_mm p_evac pv_mm rd_ready ob_ready obt_mm obh_ready obl_ready
            f_tap0 f_conv f_silu v_tap0 v_conv a_f a_hi a_lo d_mm g_sig g_ready u_gelu v_gelu v_neg v_ssq v_sd
            v_n1 v_n2 wt_mm wt_ready m_mm m_b m_u m_hi m_lo lm_mm lm_x lm_sq lv_mm lv_v lv_sd lv_d lv_R lv_n
            lv_s lv_h lv_l r_relu r_sq fin_mm fin_evac sgu_loaded""".split()
        s = {n: sem(n) for n in names}

        w_loaded = [sem(f"w_loaded{i}") for i in range(2)]
        st_free = [sem(f"st_free{i}") for i in range(4)]
        ch_loaded = [sem(f"ch_loaded{i}") for i in range(2)]
        pair_loaded = sem("pair_loaded")
        x_back = [sem(f"x_back{i}") for i in range(2)]
        out_stored = [sem(f"out_stored{i}") for i in range(2)]

        def end_phase(eng, n):
            eng.drain().then_inc(s["phase_end"], 1)
            eng.wait_ge(s["phase_end"], 5 * n)

        w_in, w_out, w_up, w_down = a["w_in"][0], a["w_out"][0], a["w_up"][0], a["w_down"][0]
        w_in2, w_out2, w_ff1, w_ff2 = a["w_in_2"][0], a["w_out_2"][0], a["w_ff1_2"][0], a["w_ff2_2"][0]

        def cols(w, c):
            return w.rearrange("(k p) n -> p k n", p=P)[:, :, bass.ds(c, P)]

        def rows(w, r):
            return w[bass.ds(r, P), :]

        ORDER = ["values", "turn_back", ("scores", 0), "pairs", "mix", "invert", ("scores", 1), ("weigh", 1)]
        for l in range(1, LEVELS):
            ORDER += [("corner", l), ("scores", l + 1), ("join", l), ("weigh", l + 1)]
        ORDER += ["begin", "read", ("weigh", 8), "solve", ("weigh", 9), "update", "load", "heads", "gram", "root"]

        def turns(eng, turn):
            for p in range(2):
                turn(0, p, p == 0, False)
            with eng.Fori(1, TT // 2 - 1) as i:
                for p in range(2):
                    turn(i, p, False, False)
            for p in range(2):
                turn(TT // 2 - 1, p, False, p == 1)

        block = ctx.enter_context(nc.Block())

        @block.sync
        def _(sp):
            def load(k, src, m=0, i=0, down=False):
                if k >= 2:
                    sp.wait_ge(s["w_lo"], k - 1 + m * i)
                dst = raw[:, k % 2] if down else raw[:, k % 2].rearrange("p (k n) -> p k n", k=KT)
                sp.dma_start(dst, src).then_inc(w_loaded[k % 2], 16)

            sp.dma_start(xin[:], a["x"][0].rearrange("(t p) d -> p t d", p=P)).then_inc(s["xin_loaded"], 16)
            for dst, src in ((ident, a["c_ident"]), (triu, a["c_triu"])):
                sp.dma_start(dst[:], src).then_inc(s["const_loaded"], 16)
            n = 0
            for name, lo in (("norm1_w", C_N1), ("norm2_w", C_N2), ("final_norm_w", C_NF), ("norm1_g_2", C_M1),
                             ("norm2_g_2", C_M2), ("final_g_2", C_MF)):
                v = a[name] if len(a[name].shape) == 1 else a[name][0]
                sp.dma_start(pack[lo:lo + 8, 0], v.rearrange("(r p) -> r p", p=P)).then_inc(s["pack_loaded"], 16)
            sp.dma_start(pack[C_CONV:C_CONV + 48, 0],
                         a["conv_qkv_w"][0].rearrange("a (r p) -> (a r) p", p=P)).then_inc(s["pack_loaded"], 16)
            for name, lo in (("conv_b_2", C_CB), ("conv_ln_g_2", C_LG), ("conv_ln_b_2", C_LB)):
                sp.dma_start(pack[lo:lo + 4, 0], a[name][0].rearrange("(r p) -> r p", p=P)).then_inc(s["pack_loaded"], 16)
            sp.dma_start(pack[C_GN:C_GN + 1, 0], a["gdn_norm_w"]).then_inc(s["pack_loaded"], 16)
            ff = a["ffn_conv_w"][0].rearrange("a (r p) -> (a r) p", p=P)
            sp.dma_start(pack[0:88, 1], ff[0:88, :]).then_inc(s["pack_loaded"], 16)
            sp.dma_start(pack[0:44, 2], ff[88:132, :]).then_inc(s["pack_loaded"], 16)
            sp.dma_start(pack[0:124, 3], a["conv_w_2"][0].rearrange("a (r p) -> (a r) p", p=P)).then_inc(s["pack_loaded"], 16)
            for dst, src in ((small[:, 0:4], a["dt_bias"][0]), (small[:, 4:8], a["a_log"][0])):
                sp.dma_start(dst, src.partition_broadcast(P)).then_inc(s["rows_loaded"], 16)
            sp.dma_start(baw[:], w_in.rearrange("(k p) n -> p k n", p=P)[:, :, 2048:2056]).then_inc(s["ba_loaded"], 16)

            for n in range(12):
                load(U_QKVB + n, cols(w_in, 2056 + P * n))
            with sp.Fori(0, 3) as i:
                for u in range(4):
                    load(U_QKV + u, cols(w_in, (4 * i + u) * P), 4, i)
            for n in range(4):
                load(U_Z + n, cols(w_in, 1536 + P * n))
            end_phase(sp, 1)

            sp.dma_start(strip[:], a["c_strip"]).then_inc(s["mask_loaded"], 16)
            sp.dma_start(lmask[:], a["c_levels"]).then_inc(s["mask_loaded"], 16)
            for n in range(2):
                load(U_OUT1 + n, cols(w_out, P * n))

            def chunk(c):
                sp.dma_start(ch[:, c % 2], qkvz_s[:, :, c * P:(c + 1) * P]).then_inc(ch_loaded[c % 2], 16)

            def pair(t):
                sp.dma_start(qkvb[:], qkvb_s.rearrange("p (m t) s -> p m t s", m=3)[:, :, t, :]).then_inc(pair_loaded, 16)

            chunk(0)
            pair(0)
            chunk(1)
            for i in range(1, 4):
                sp.wait_ge(s["og_ready"], 2 * i - 1)
                chunk(2 * i)
                sp.wait_ge(s["s_mm"], 16 * i)
                pair(i)
                sp.wait_ge(s["og_ready"], 2 * i)
                chunk(2 * i + 1)
            end_phase(sp, 2)

            for m in range(2):
                sp.dma_start(x[:, 4 * m:4 * m + 4], x_s[:, 4 * m:4 * m + 4]).then_inc(x_back[m], 16)
            for n in range(2, 4):
                load(U_OUT1 + n, cols(w_out, P * n))
            for n in range(4, 8):
                load(U_OUT1 + n, cols(w_out, P * n))

            F = U_FFN1
            load(F, cols(w_up, 0))
            load(F + 1, cols(w_up, FF1 * P))
            with sp.Fori(0, (FF1 - 2) // 2) as i:
                for u in range(2):
                    j = 2 * i + 1 + u
                    load(F + 2 + 3 * u, cols(w_up, j * P), 6, i)
                    load(F + 3 + 3 * u, cols(w_up, (j + FF1) * P), 6, i)
                    load(F + 4 + 3 * u, rows(w_down, (j - 1) * P), 6, i, down=True)
            load(U_IN2 - 4, cols(w_up, (FF1 - 1) * P))
            load(U_IN2 - 3, cols(w_up, (2 * FF1 - 1) * P))
            load(U_IN2 - 2, rows(w_down, (FF1 - 2) * P), down=True)
            load(U_IN2 - 1, rows(w_down, (FF1 - 1) * P), down=True)

            with sp.Fori(0, 2) as i:
                for u in range(4):
                    load(U_IN2 + u, cols(w_in2, 1024 + 512 * (u % 2) + (2 * i + u // 2) * P), 4, i)
            for n in range(4):
                load(U_IN2 + 8 + n, cols(w_in2, P * n))
            for n in range(4):
                load(U_IN2 + 12 + n, cols(w_in2, 512 + P * n))
            sp.wait_ge(s["g_ready"], 1)
            sp.dma_start(bsb[:], a["sgu_b_2"][0].partition_broadcast(P)).then_inc(s["sgu_loaded"], 16)
            sp.dma_start(lng[:], a["sgu_ln_g_2"][0].partition_broadcast(P)).then_inc(s["sgu_loaded"], 16)
            sp.dma_start(lnb[:], a["sgu_ln_b_2"][0].partition_broadcast(P)).then_inc(s["sgu_loaded"], 16)
            sp.dma_start(sgw[:, 0], a["sgu_w_2"][0].rearrange("h t s -> t h s")).then_inc(s["sgu_loaded"], 16)
            for n in range(8):
                load(U_OUT2 + n, cols(w_out2, P * n))
            F = U_FFN2
            load(F, cols(w_ff1, 0))
            with sp.Fori(0, (FF2 - 2) // 2) as i:
                for u in range(2):
                    j = 2 * i + 1 + u
                    load(F + 1 + 2 * u, cols(w_ff1, j * P), 4, i)
                    load(F + 2 + 2 * u, rows(w_ff2, (j - 1) * P), 4, i, down=True)
            load(U_END - 3, cols(w_ff1, (FF2 - 1) * P))
            load(U_END - 2, rows(w_ff2, (FF2 - 2) * P), down=True)
            load(U_END - 1, rows(w_ff2, (FF2 - 1) * P), down=True)

            for t in range(TT):
                sp.wait_ge(s["fin_evac"], t + 1)
                sp.dma_start(out[0, t * P:(t + 1) * P, :], hf[:, t % 2]).then_inc(out_stored[t % 2], 16)
            for b in range(2):
                sp.wait_ge(out_stored[b], 16 * (TT // 2))

        @block.gpsimd
        def _(pool):
            nc.gpsimd.memset(ones[:], 1.0).then_inc(s["consts_set"], 1)
            pool.wait_ge(s["const_loaded"], 32)
            pool.wait_ge(s["x_written"], KT)
            pool.dma_start(x_s, x[:]).then_inc(s["x_spilled"], 16)
            for n in range(12):
                pool.wait_ge(s["st_written"], n + 1)
                pool.dma_start(qkvb_s[:, n], st[:, n % 4]).then_inc(st_free[n % 4], 16)
            with pool.Fori(0, 3) as i:
                for u in range(4):
                    pool.wait_ge(s["st_written"], 13 + u + 4 * i)
                    pool.dma_start(qkvz_s[:, bass.ds(4 * i + u, 1), :], st[:, u:u + 1]).then_inc(st_free[u], 16)
            for n in range(4):
                pool.wait_ge(s["st_written"], U_Z + n + 1)
                pool.dma_start(qkvz_s[:, 12 + n], st[:, n]).then_inc(st_free[n], 16)
            for b in range(4):
                pool.wait_ge(st_free[b], 16 * 7)
            pool.wait_ge(s["x_spilled"], 16)
            end_phase(pool, 1)

            PT = nc.gpsimd.tensor_tensor
            nc.gpsimd.memset(G["St"][:], 0.0).then_inc(s["s_ready"], 1)

            def begin(c, p):
                cp = cc[:, p]
                pool.wait_ge(s["cc_ready"], c + 1)
                PT(G["U"][:], again(triu[:], GH), first(cp[:, T_G:T_G + 4], P), ALU.mult).then_inc(s["tri_ready"], 1)
                PT(G["bm"][:], again(triu[:], GH), first(cp[:, T_BETA:T_BETA + 4], P), ALU.mult).then_inc(s["tri_ready"], 1)

            begin(0, 0)

            def turn(i, p, first_chunk, last):
                c = 2 * i + p
                for stage in ORDER:
                    if stage == "invert":
                        pool.wait_ge(s["lat_ready"], 2 * c + 1)
                        PT(G["TT"][:], G["LT"][:], again(lmask[:, 0], GH), ALU.mult).then_inc(s["tt0_raw"], 1)
                        pool.wait_ge(s["tt0_raw"], c + 1)
                        PT(G["TT"][:], again(ident[:], GH), G["TT"][:], ALU.subtract).then_inc(s["tt0_ready"], 1)
                        pool.wait_ge(s["gam_ready"], c + 1)
                        pool.wait_ge(s["kqT_ready"], 2 * c + 2)
                        PT(G["kd"][:], G["knT"][:], G["gam"][:], ALU.mult).then_inc(s["kqd_ready"], 1)
                        PT(G["qd"][:], G["qnT"][:], G["gam"][:], ALU.mult).then_inc(s["kqd_ready"], 1)
                        pool.wait_ge(s["eb_ready"], c + 1)
                        PT(G["ke"][:], G["kn"][:], G["E"][:, :, P - 1:P].broadcast_to([P, GH, P]), ALU.mult)\
                            .then_inc(s["ke_ready"], 1)
                        pool.wait_ge(s["s_ready"], c + 1)
                        PT(G["Sg"][:], G["St"][:], G["gam"][:, :, P - 1:P].broadcast_to([P, GH, P]), ALU.mult)\
                            .then_inc(s["sg_ready"], 1)
                    elif stage == "begin" and not last:
                        pool.wait_ge(s["lev_w"], 6 * c + 6)
                        begin(c + 1, 1 - p)
                    elif stage == "root":
                        pool.wait_ge(s["o_copied"], c + 1)
                        pool.wait_ge(s["o_r"], c + 1)
                        PT(G["oz"][:], G["oz"][:], first(oc[:, 3], P), ALU.mult).then_inc(s["on_ready"], 1)

            turns(pool, turn)
            end_phase(pool, 2)

            pool.wait_ge(s["sgu_loaded"], 64)
            for t in range(TT):
                pool.wait_ge(s["v_n1"], t + 1)
                nc.gpsimd.tensor_tensor(vt[:, t], vt[:, t], lng[:], ALU.mult).then_inc(s["v_n2"], 1)
                pool.wait_ge(s["v_n2"], 2 * t + 1)
                nc.gpsimd.tensor_tensor(vt[:, t], vt[:, t], lnb[:], ALU.add).then_inc(s["v_n2"], 1)

        @block.scalar
        def _(act):
            A = nc.scalar.activation

            def prep(k, slot, m=0, i=0):
                act.wait_ge(w_loaded[k % 2], 16 * (k // 2 + 1) + 8 * m * i)
                if k >= 4:
                    act.wait_ge(s["w_used"], k - 3 + m * i)
                A(whs(slot), raw[:, k % 2], ACT.Copy).then_inc(s["w_hi"], 1)

            def square(r, k, xbase):
                act.wait_ge(s["x_written"], xbase + k + 1)
                if k >= 3:
                    act.wait_ge(s["n_acc"], 7 * r + k - 2)
                A(sqt[:, k % 2] if k else nacc[:], x[:, k], ACT.Square).then_inc(s["n_sq"], 1)

            def norm_root(r):
                act.wait_ge(s["n_v"], r + 1)
                A(small[:, 16:24], small[:, 8:16], ACT.Sqrt).then_inc(s["n_sd"], 1)

            def norm_stats(r, xbase):
                for k in range(KT):
                    square(r, k, xbase)
                norm_root(r)

            def norm_halves(q):
                for k in range(KT):
                    act.wait_ge(s["n_x"], KT * q + k + 1)
                    A(hh[:, k], hf[:, k % 2], ACT.Copy).then_inc(s["n_hi"], 1)

            prep(0, 0)
            norm_stats(0, 0)
            norm_halves(0)
            prep(1, 1)
            act.wait_ge(s["ba_loaded"], 16)
            A(bah[:], baw[:], ACT.Copy).then_inc(s["ba_hi"], 1)

            for n in range(12):
                prep(n + 2, (n + 2) % 4)
                act.wait_ge(s["w_used"], n + 1)
                if n >= 4:
                    act.wait_ge(st_free[n % 4], 16 * (n // 4))
                A(st[:, n % 4], acc(n % 2), ACT.Copy, scale=(0.125 if n < 4 else 1.0)).then_inc(s["st_written"], 1)
            act.wait_ge(s["st_written"], 12)
            A(sqb[:], st[:, 3], ACT.Square).then_inc(s["sq_init"], 1)
            with act.Fori(0, 3) as i:
                for u in range(4):
                    prep(U_QKV + u + 2, (u + 2) % 4, 4, i)
                    act.wait_ge(s["w_used"], U_QKV + u + 1 + 4 * i)
                    A(cacc[:, u % 2], acc(u % 2), ACT.Copy,
                      scale=par[:, bass.ds(C_CONV + 36 + 4 * i + u, 1)]).then_inc(s["tap0"], 1)
                    act.wait_ge(s["conv"], 12 * i + 3 * u + 3)
                    act.wait_ge(st_free[u], 48 + 16 * i)
                    A(st[:, u], cacc[:, u % 2], ACT.Silu).then_inc(s["silu"], 1)
                    act.wait_ge(s["silu"], 4 * i + u + 1)
                    act.wait_ge(s["col_mm"], 4 * i + u + 1)
                    A(sqb[:], st[:, u], ACT.Square).then_inc(s["st_written"], 1)
            for n in range(4):
                if n < 2:
                    prep(U_Z + n + 2, n + 2)
                act.wait_ge(s["w_used"], U_Z + n + 1)
                act.wait_ge(st_free[n], 96)
                A(st[:, n], acc(n % 2), ACT.Silu).then_inc(s["st_written"], 1)
            end_phase(act, 1)

            act.wait_ge(s["rows_loaded"], 32)
            act.wait_ge(s["tab_dve"], 1)
            A(tmpt[:, 1], tmpt[:, 0], ACT.Sqrt).then_inc(s["tab_act"], 1)
            act.wait_ge(s["tab_dve"], 2)
            A(tmpt[:, 3, 0:32], tmpt[:, 2, 0:32], ACT.Sigmoid).then_inc(s["tab_act"], 1)
            A(tmpt[:, 5, 0:32], tmpt[:, 4, 32:64], ACT.Exp, scale=-1.0).then_inc(s["tab_act"], 1)
            A(small[:, 24:28], small[:, 4:8], ACT.Exp).then_inc(s["tab_act"], 1)
            for n in range(2):
                prep(U_OUT1 + n, n)

            def load(c):
                act.wait_ge(s["gc_mm"], c + 1)
                A(G["gam"][:], heads(0), ACT.Exp).then_inc(s["gam_ready"], 1)

            def gram(c):
                act.wait_ge(s["d_ready"], c + 1)
                A(G["E"][:], G["E"][:], ACT.Exp).then_inc(s["e_ready"], 1)
                act.wait_ge(s["v_mm"], c + 1)
                A(G["v"][:], heads(0), ACT.Copy).then_inc(s["v_ready"], 1)

            def mix(c):
                act.wait_ge(s["og_ready"], c + 1)
                A(hh[:, 0:GH, bass.ds(c * P, P)], G["og"][:], ACT.Copy).then_inc(s["oh_ready"], 1)

            act.sem_inc(s["p_evac"], 2)
            load(0)
            gram(0)

            def turn(i, p, first_chunk, last):
                c = 2 * i + p
                g0 = 24 * i + 12 * p
                for stage in ORDER:
                    if stage == "values" and p == 0:
                        act.wait_ge(s["vt_mm"], i + 1)
                        A(vb[:].rearrange("p t d -> p (t d)"), PS[:, 3:5, :].rearrange("p a b -> p (a b)"), ACT.Copy)\
                            .then_inc(s["vb_ready"], 1)
                    elif stage == "turn_back":
                        act.wait_ge(s["kqT_mm"], 2 * c + 1)
                        A(G["knT"][:], heads(1), ACT.Copy).then_inc(s["kqT_ready"], 1)
                        act.wait_ge(s["kqT_mm"], 2 * c + 2)
                        A(G["qnT"][:], heads(2), ACT.Copy).then_inc(s["kqT_ready"], 1)
                    elif stage == "solve":
                        act.wait_ge(s["u_mm"], c + 1)
                        A(G["u"][:], heads(1), ACT.Copy).then_inc(s["u_ready"], 1)
                    elif stage == "update":
                        act.wait_ge(s["os_mm"], 2 * c + 1)
                        A(G["oz"][:], heads(2), ACT.Copy).then_inc(s["o_copied"], 1)
                        act.wait_ge(s["o_copied"], c + 1)
                        A(G["v"][:], G["oz"][:], ACT.Square).then_inc(s["osq"], 1)
                    elif stage == "load" and not last:
                        load(c + 1)
                    elif stage == "heads" and p == 1:
                        act.wait_ge(s["obt_mm"], i + 1)
                        A(hh[:, bass.ds(4 + i, 1), :].rearrange("p a s -> p (a s)"),
                          PS[:, 3:5, :].rearrange("p a b -> p (a b)"), ACT.Copy).then_inc(s["obh_ready"], 1)
                    elif stage == "gram" and not last:
                        act.wait_ge(s["oss"], c + 1)
                        gram(c + 1)
                    elif stage == "root":
                        act.wait_ge(s["o_v"], c + 1)
                        A(oc[:, 2], oc[:, 1], ACT.Sqrt).then_inc(s["o_sd"], 1)
                    elif stage == "mix" and not first_chunk:
                        mix(c - 1)
                    elif stage[0] == "scores" and stage[1] < 8:
                        h, n = stage[1], P * (stage[1] + 1)
                        act.wait_ge(s["s_neg"], 16 * i + 8 * p + h + 1)
                        A(sm[:, h % 2, 0:n], sm[:, h % 2, 0:n], ACT.Exp, bias=ac[:, 1, 8 * p + h:8 * p + h + 1],
                          accum_out=ac[:, 2, 8 * p + h:8 * p + h + 1]).then_inc(s["s_exp"], 1)
                    elif stage[0] == "weigh" and stage[1] <= 8:
                        for g, n in groups(stage[1] - 1):
                            act.wait_ge(s["p_mm"], g0 + g + 1)
                            act.wait_ge(s["pv_mm"], g0 + g + 1)
                            A(pt[:, g % 2, 0:n * P], PS[:, 5 + g % 2, 0:n * P], ACT.Copy).then_inc(s["p_evac"], 1)

            turns(act, turn)
            mix(TT - 1)
            end_phase(act, 2)

            for n in range(8):
                prep(U_OUT1 + n + 2, (n + 2) % 4)
                if n:
                    square(1, n - 1, X_OUT1)
            square(1, KT - 1, X_OUT1)
            norm_root(1)
            norm_halves(1)

            F = U_FFN1

            def last_tap(dst, col, name, k, bank, m=0, i=0):
                act.wait_ge(s["w_used"], k + 1 + m * i)
                A(dst[:], acc(bank), ACT.Copy, scale=par[:, bass.ds(col, 1)]).then_inc(s[name], 1)

            def gate_silu(j):
                act.wait_ge(s["f_conv"], 2 * j + 2)
                A(gc[:], gc[:], ACT.Silu).then_inc(s["f_silu"], 1)

            def high_a(count, b, used):
                act.wait_ge(s["a_f"], count)
                act.wait_ge(s["w_used"], used)
                A(fh[:, b], uc[:], ACT.Copy).then_inc(s["a_hi"], 1)

            prep(F + 2, 2)
            last_tap(gc, C_FF2, "f_tap0", F, 0)
            prep(F + 3, 3)
            gate_silu(0)
            with act.Fori(0, (FF1 - 2) // 2) as i:
                for u in range(2):
                    j = 2 * i + 1 + u
                    g = F + 2 + 3 * u
                    prep(g + 2, (g + 2 - F) % 6, 6, i)
                    last_tap(uc, C_FF2 + FF1 - 1 + j, "v_tap0", g - 2 if u else F + 1, 1, 6, i)
                    high_a(j, u, g - 3 + 6 * i)
                    prep(g + 3, (g + 3 - F) % 6, 6, i)
                    last_tap(gc, C_FF2 + j, "f_tap0", g, 0, 6, i)
                    gate_silu(j)
                    prep(g + 4, (g + 4 - F) % 6, 6, i)
            g = U_IN2 - 4
            prep(g + 2, (g + 2 - F) % 6)
            last_tap(uc, C_FF2 + 2 * FF1 - 2, "v_tap0", g - 2, 1)
            high_a(FF1 - 1, 0, g - 3)
            prep(g + 3, (g + 3 - F) % 6)
            last_tap(gc, C_FF2 + FF1 - 1, "f_tap0", g, 0)
            gate_silu(FF1 - 1)
            last_tap(uc, C_FF2 + 2 * FF1 - 1, "v_tap0", g + 1, 1)
            high_a(FF1, 1, g)
            prep(U_IN2, 0)
            norm_stats(2, X_FFN1 + KT * (FF1 - 1))
            norm_stats(3, X_MID)
            norm_halves(2)
            prep(U_IN2 + 1, 1)

            V = U_IN2
            for n in range(8):
                prep(V + n + 2, (n + 2) % 4)
                if n % 2:
                    act.wait_ge(s["w_used"], V + n + 1)
                    if n > 1:
                        act.wait_ge(s["g_ready"], n // 2)
                    A(sgb[:], acc(2 * (n // 2 % 2) + 1), ACT.Sigmoid).then_inc(s["g_sig"], 1)
            for h in range(GH):
                prep(V + 10 + h, (10 + h) % 4)
                act.wait_ge(s["w_used"], V + 9 + h)
                A(ub[:, h], acc(h % 2), ACT.Gelu).then_inc(s["u_gelu"], 1)
            for n in (14, 15):
                prep(V + n, n % 4)
            for t in range(TT):
                act.wait_ge(s["m_mm"], t + 1)
                A(vt[:, t], PS[:, 4 + t % 4, :], ACT.Gelu, accum_out=small[:, 32 + t:33 + t]).then_inc(s["v_gelu"], 1)
            act.wait_ge(s["v_neg"], 1)
            for t in range(TT):
                if t:
                    act.wait_ge(s["v_ssq"], t)
                A(sgb[:, 0:HALF], vt[:, t], ACT.Square, bias=small[:, 40 + t:41 + t],
                  accum_out=small[:, 48 + t:49 + t]).then_inc(s["v_ssq"], 1)
            act.wait_ge(s["v_neg"], 2)
            A(small[:, 64:72], small[:, 56:64], ACT.Sqrt).then_inc(s["v_sd"], 1)
            for t in range(TT):
                act.wait_ge(s["m_u"], t + 1)
                A(hh[:, 0:GH, t * P:(t + 1) * P], sgb[:, (t % 2) * HALF:(t % 2 + 1) * HALF].rearrange("p (h t) -> p h t", h=GH),
                  ACT.Copy).then_inc(s["m_hi"], 1)
            for q in range(4):
                act.wait_ge(s["lm_x"], q + 1)
                A(ub[:, q], cg[:, q], ACT.Square).then_inc(s["lm_sq"], 1)
            act.wait_ge(s["lv_v"], 1)
            A(small[:, 128:160], small[:, 96:128], ACT.Sqrt).then_inc(s["lv_sd"], 1)
            for q in range(4):
                act.wait_ge(s["lv_n"], q + 1)
                A(cg[:, q], cg[:, q], ACT.Silu, scale=par[:, C_LG + q:C_LG + q + 1],
                  bias=par[:, C_LB + q:C_LB + q + 1]).then_inc(s["lv_s"], 1)
                act.wait_ge(s["lv_s"], q + 1)
                A(hh[:, 4 + q], cg[:, q], ACT.Copy).then_inc(s["lv_h"], 1)
            for n in range(2):
                prep(U_OUT2 + n, n)
            for n in range(8):
                prep(U_OUT2 + n + 2, (n + 2) % 4)
                if n:
                    square(4, n - 1, X_OUT2)
            square(4, KT - 1, X_OUT2)
            norm_root(4)
            norm_halves(3)
            F = U_FFN2

            def relu_square(j, b):
                A(gc[:], acc(b), ACT.Relu).then_inc(s["r_relu"], 1)
                act.wait_ge(s["r_relu"], j + 1)
                act.wait_ge(s["a_lo"], FF1 + j)
                A(uc[:], gc[:], ACT.Square).then_inc(s["r_sq"], 1)
                act.wait_ge(s["r_sq"], j + 1)
                A(fh[:, b], uc[:], ACT.Copy).then_inc(s["a_hi"], 1)

            prep(F + 2, 2)
            act.wait_ge(s["w_used"], F + 1)
            relu_square(0, 0)
            with act.Fori(0, (FF2 - 2) // 2) as i:
                for u in range(2):
                    up = F + 1 + 2 * u
                    prep(up + 2, (3 + 2 * u) % 4, 4, i)
                    act.wait_ge(s["w_used"], up + 1 + 4 * i)
                    relu_square(2 * i + 1 + u, 1 - u)
                    prep(up + 3, (4 + 2 * u) % 4, 4, i)
            prep(U_END - 1, 3)
            act.wait_ge(s["w_used"], U_END - 2)
            relu_square(FF2 - 1, 1)
            norm_stats(5, X_FFN2 + KT * (FF2 - 1))
            for t in range(TT):
                act.wait_ge(s["fin_mm"], t + 1)
                if t >= 2:
                    act.wait_ge(out_stored[t % 2], 16 * (t // 2))
                A(hf[:, t % 2], acc(t % 4), ACT.Copy).then_inc(s["fin_evac"], 1)

        @block.vector
        def _(dve):
            V_ = nc.vector
            TTo, STT, TS = V_.tensor_tensor, V_.scalar_tensor_tensor, V_.tensor_scalar
            chain = [0]

            def done(ins):
                chain[0] += 1
                ins.then_inc(s["v_chain"], 1)
                dve.wait_ge(s["v_chain"], chain[0])

            def prep(k, slot, m=0, i=0):
                dve.wait_ge(s["w_hi"], k + 1 + m * i)
                TTo(wls(slot), raw[:, k % 2], whs(slot).bitcast(F32), ALU.subtract).then_inc(s["w_lo"], 1)

            def add_square(r, k):
                if k < 1:
                    return
                dve.wait_ge(s["n_sq"], KT * r + k + 1)
                if k > 1:
                    dve.wait_ge(s["n_acc"], 7 * r + k - 1)
                TTo(nacc[:], nacc[:], sqt[:, k % 2], ALU.add).then_inc(s["n_acc"], 1)

            def norm_factor(r):
                dve.wait_ge(s["n_cols"], r + 1)
                TS(small[:, 8:16], PS[:, 5, 0:8], 1.0 / D, EPS, ALU.mult, ALU.add).then_inc(s["n_v"], 1)
                dve.wait_ge(s["n_sd"], r + 1)
                done(V_.reciprocal(small[:, 24:32], small[:, 16:24]))
                TTo(diag[:], again(ident[:], TT), first(small[:, 24:32], P), ALU.mult).then_inc(s["n_diag"], 1)
                dve.wait_ge(s["n_R"], r + 1)

            def norm_halves(q, col):
                for k in range(KT + 1):
                    if k < KT:
                        if k >= 2:
                            dve.wait_ge(s["n_lo"], KT * q + k - 1)
                        STT(hf[:, k % 2], x[:, k], par[:, col + k:col + k + 1], acc(3), ALU.mult, ALU.mult).then_inc(s["n_x"], 1)
                    if k:
                        dve.wait_ge(s["n_hi"], KT * q + k)
                        TTo(hl[:, k - 1], hf[:, (k - 1) % 2], hh[:, k - 1].bitcast(F32), ALU.subtract).then_inc(s["n_lo"], 1)

            def norm_in_place(col, r=None):
                for k in range(KT):
                    STT(x[:, k], x[:, k], par[:, col + k:col + k + 1], acc(3), ALU.mult, ALU.mult).then_inc(s["x_written"], 1)
                    if r is not None:
                        add_square(r, k - 1)
                if r is not None:
                    add_square(r, KT - 1)

            dve.wait_ge(s["const_loaded"], 32)
            dve.wait_ge(s["par_mm"], 1)
            V_.tensor_copy(par[:, 0:109], PS[:, 4, 0:109]).then_inc(s["par_ready"], 1)
            V_.tensor_copy(par[:, 128:216], PS[:, 4, 128:216]).then_inc(s["par_ready"], 1)
            V_.tensor_copy(par[:, 256:300], PS[:, 4, 256:300]).then_inc(s["par_ready"], 1)
            V_.tensor_copy(par[:, 384:508], PS[:, 4, 384:508]).then_inc(s["par_ready"], 1)
            for k in range(KT):
                dve.wait_ge(s["xt_mm"], k + 1)
                V_.tensor_copy(x[:, k], acc(k % 2)).then_inc(s["x_written"], 1)
                add_square(0, k - 1)
            add_square(0, KT - 1)
            prep(0, 0)
            norm_factor(0)
            dve.wait_ge(s["par_ready"], 4)
            norm_halves(0, C_N1)
            prep(1, 1)
            dve.wait_ge(s["ba_hi"], 1)
            TTo(bal[:], baw[:], bah[:].bitcast(F32), ALU.subtract).then_inc(s["ba_lo"], 1)

            for n in range(12):
                prep(n + 2, (n + 2) % 4)
            with dve.Fori(0, 3) as i:
                for u in range(4):
                    prep(U_QKV + u + 2, (u + 2) % 4, 4, i)
                    dve.wait_ge(s["tap0"], 4 * i + u + 1)
                    for d in range(1, 4):
                        if d > 1:
                            dve.wait_ge(s["conv"], 12 * i + 3 * u + d - 1)
                        STT(cacc[:, u % 2, d:S], acc(u % 2)[:, 0:S - d],
                            par[:, bass.ds(C_CONV + 12 * (3 - d) + 4 * i + u, 1)], cacc[:, u % 2, d:S],
                            ALU.mult, ALU.add).then_inc(s["conv"], 1)
            prep(U_Z + 2, 2)
            prep(U_Z + 3, 3)
            end_phase(dve, 1)

            dve.wait_ge(s["rows_loaded"], 32)
            TS(tmpt[:, 0].rearrange("p (t c) -> p t c", c=8), PS[:, 7, 0:96].rearrange("p (t c) -> p t c", c=12)[:, :, 1:9],
               EPS, None, ALU.add).then_inc(s["tab_dve"], 1)
            ba = PS[:, 6, 0:64].rearrange("p (t c) -> p t c", c=8)
            done(TTo(tmpt[:, 4, 0:32].rearrange("p (t c) -> p t c", c=4), ba[:, :, 4:8], again(small[:, 0:4], TT), ALU.add))
            done(V_.tensor_copy(tmpt[:, 2, 0:32].rearrange("p (t c) -> p t c", c=4), ba[:, :, 0:4]))
            STT(tmpt[:, 4, 32:64], tmpt[:, 4, 0:32], -1.0, tmpt[:, 4, 0:32], ALU.mult, ALU.max).then_inc(s["tab_dve"], 1)
            dve.wait_ge(s["tab_act"], 4)
            done(V_.reciprocal(tmpt[:, 6], tmpt[:, 1]))
            rn = tmpt[:, 6].rearrange("p (t c) -> p t c", c=8)
            TS(tab[:, :, T_RQ:T_RQ + 4], rn[:, :, 0:4], float(P) ** -0.5, None, ALU.mult)
            V_.tensor_copy(tab[:, :, T_RK:T_RK + 4], rn[:, :, 4:8])
            V_.tensor_copy(tab[:, :, T_BETA:T_BETA + 4], tmpt[:, 3, 0:32].rearrange("p (t c) -> p t c", c=4))
            e, w, zz, z2, pl = tmpt[:, 5, 0:32], tmpt[:, 5, 32:64], tmpt[:, 7, 0:32], tmpt[:, 7, 32:64], tmpt[:, 3, 32:64]
            done(TS(w, e, 2.0, None, ALU.add))
            done(V_.reciprocal(w, w))
            done(TTo(zz, e, w, ALU.mult))
            done(TTo(z2, zz, zz, ALU.mult))
            done(TS(pl, z2, 1.0 / 17, None, ALU.mult))
            for n in (15, 13, 11, 9, 7, 5, 3):
                done(STT(pl, pl, 1.0 / n, z2, ALU.add, ALU.mult))
            done(STT(pl, pl, 1.0, zz, ALU.add, ALU.mult))
            done(TS(w, tmpt[:, 4, 0:32], 0.0, None, ALU.max))
            done(STT(pl, pl, 2.0, w, ALU.mult, ALU.add))
            done(STT(tab[:, :, T_G:T_G + 4], pl.rearrange("p (t c) -> p t c", c=4), -1.0,
                     again(small[:, 24:28], TT), ALU.mult, ALU.mult))
            dve.sem_inc(s["tab_dve"], 1)
            dve.wait_ge(s["tab_mm"], 1)
            done(TS(tab[:, :, T_NGC:T_NGC + 4], PS[:, 5, 0:32].rearrange("p (t c) -> p t c", c=4), -1.0, None, ALU.mult))
            for n in range(2):
                prep(U_OUT1 + n, n)
            dve.wait_ge(s["mask_loaded"], 32)

            dve.sem_inc(s["s_max"], 1)
            dve.sem_inc(s["ob_ready"], 1)
            dve.sem_inc(s["obl_ready"], 1)

            def begin(c, p):
                V_.tensor_copy(cc[:, p], tab[:, bass.ds(c, 1), :].rearrange("p a n -> p (a n)")).then_inc(s["cc_ready"], 1)

            def load(c, p):
                dve.wait_ge(s["cc_ready"], c + 1)
                dve.wait_ge(s["gam_ready"], c + 1)
                TTo(G["E"][:], heads(0), first(cc[:, p, T_NGC:T_NGC + 4], P), ALU.add).then_inc(s["d_raw"], 1)
                dve.wait_ge(s["d_raw"], c + 1)
                TS(G["E"][:], G["E"][:], 0.0, None, ALU.min).then_inc(s["d_ready"], 1)

            def gram(c, p):
                dve.wait_ge(s["kq_mm"], 2 * c + 1)
                TTo(G["kn"][:], heads(1), first(cc[:, p, T_RK:T_RK + 4], P), ALU.mult).then_inc(s["kqn_ready"], 1)
                dve.wait_ge(s["kq_mm"], 2 * c + 2)
                TTo(G["qn"][:], heads(2), first(cc[:, p, T_RQ:T_RQ + 4], P), ALU.mult).then_inc(s["kqn_ready"], 1)

            def mix(c, p):
                dve.wait_ge(s["ot_mm"], c + 1)
                STT(G["og"][:], heads(7), par[:, C_GN:C_GN + 1], ch[:, p, 12:16], ALU.mult, ALU.mult)\
                    .then_inc(s["og_ready"], 1)

            def mix_low(c):
                dve.wait_ge(s["oh_ready"], c + 1)
                TTo(hl[:, 0:GH, bass.ds(c * P, P)], G["og"][:], hh[:, 0:GH, bass.ds(c * P, P)].bitcast(F32),
                    ALU.subtract).then_inc(s["ol_ready"], 1)

            begin(0, 0)
            load(0, 0)
            gram(0, 0)

            def turn(i, p, first_chunk, last):
                c = 2 * i + p
                g0 = 24 * i + 12 * p
                for stage in ORDER:
                    if stage == "turn_back":
                        dve.wait_ge(s["e_ready"], c + 1)
                        dve.wait_ge(s["tri_ready"], 2 * c + 2)
                        TTo(G["E"][:], G["E"][:], G["bm"][:], ALU.mult).then_inc(s["eb_ready"], 1)
                    elif stage == "pairs":
                        dve.wait_ge(s["gram_mm"], 2 * c + 1)
                        dve.wait_ge(s["eb_ready"], c + 1)
                        TTo(G["LT"][:], heads(1), G["E"][:], ALU.mult).then_inc(s["lat_ready"], 1)
                        dve.wait_ge(s["gram_mm"], 2 * c + 2)
                        TTo(G["AT"][:], heads(2), G["E"][:], ALU.mult).then_inc(s["lat_ready"], 1)
                    elif stage[0] == "corner":
                        l = stage[1]
                        dve.wait_ge(s["lev_l"], 6 * c + l)
                        TTo(G["U"][:], heads(0), again(lmask[:, 1 + l], GH), ALU.mult).then_inc(s["lev_u"], 1)
                    elif stage[0] == "join":
                        l = stage[1]
                        if l < 6:
                            dve.wait_ge(s["lev_v"], 5 * c + l)
                            TTo(G["T"][:], G["T"][:], heads(1), ALU.subtract).then_inc(s["lev_t"], 1)
                        dve.wait_ge(s["lev_w"], 6 * c + l)
                        TTo(G["TT"][:], G["TT"][:], heads(2), ALU.subtract).then_inc(s["lev_tt"], 1)
                    elif stage == "begin" and not last:
                        begin(c + 1, 1 - p)
                    elif stage == "read":
                        dve.wait_ge(s["ks_mm"], c + 1)
                        dve.wait_ge(s["v_ready"], c + 1)
                        TTo(G["v"][:], G["v"][:], heads(0), ALU.subtract).then_inc(s["r_ready"], 1)
                    elif stage == "update":
                        dve.wait_ge(s["os_mm"], 2 * c + 2)
                        dve.wait_ge(s["sg_ready"], c + 1)
                        TTo(G["St"][:], G["Sg"][:], heads(0), ALU.add).then_inc(s["s_ready"], 1)
                        dve.wait_ge(s["osq"], c + 1)
                        V_.tensor_reduce(oc[:, 0], G["v"][:], AX_X, ALU.add).then_inc(s["oss"], 1)
                        dve.wait_ge(s["oss"], c + 1)
                        TS(oc[:, 1], oc[:, 0], 1.0 / P, EPS, ALU.mult, ALU.add).then_inc(s["o_v"], 1)
                    elif stage == "load" and not last:
                        load(c + 1, 1 - p)
                    elif stage == "heads" and p == 1:
                        dve.wait_ge(s["obh_ready"], i + 1)
                        TTo(hl[:, bass.ds(4 + i, 1), :].rearrange("p a s -> p (a s)"),
                            PS[:, 3:5, :].rearrange("p a b -> p (a b)"),
                            hh[:, bass.ds(4 + i, 1), :].rearrange("p a s -> p (a s)").bitcast(F32),
                            ALU.subtract).then_inc(s["obl_ready"], 1)
                    elif stage == "gram" and not last:
                        gram(c + 1, 1 - p)
                    elif stage == "root":
                        dve.wait_ge(s["o_sd"], c + 1)
                        V_.reciprocal(oc[:, 3], oc[:, 2]).then_inc(s["o_r"], 1)
                    elif stage == "mix" and not first_chunk:
                        mix(c - 1, 1 - p)
                    elif stage == "invert":
                        dve.wait_ge(s["l_mm"], c + 1)
                        TTo(G["U"][:], heads(0), again(lmask[:, 1], GH), ALU.mult).then_inc(s["u0_ready"], 1)
                        dve.wait_ge(s["u0_ready"], c + 1)
                        TTo(G["T"][:], again(ident[:], GH), G["U"][:], ALU.subtract).then_inc(s["lev_t"], 1)
                        if not first_chunk:
                            mix_low(c - 1)
                    elif stage[0] == "scores" and stage[1] < 8:
                        h, n, k = stage[1], P * (stage[1] + 1), 8 * p + stage[1]
                        dve.wait_ge(s["s_mm"], 16 * i + k + 1)
                        if h >= 2:
                            dve.wait_ge(s["p_mm"], g0 + groups(h - 2)[-1][0] + 1)
                        V_.memset(small[:, 255:256], 0.0)
                        V_.tensor_tensor_reduce(out=sm[:, h % 2, 0:n],
                                                in0=PS[:, 3:5, :].rearrange("p a b -> p (a b)")[:, 0:n],
                                                in1=strip[:, S - n:S], scale=1.0, scalar=-3e38, op0=ALU.add,
                                                op1=ALU.max, accum_out=ac[:, 0, k:k + 1]).then_inc(s["s_max"], 1)
                        dve.wait_ge(s["s_max"], 16 * i + k + 2)
                        TS(ac[:, 1, k:k + 1], ac[:, 0, k:k + 1], -1.0, None, ALU.mult).then_inc(s["s_neg"], 1)
                    elif stage[0] == "weigh" and stage[1] >= 2:
                        h, k = stage[1] - 2, 8 * p + stage[1] - 2
                        dve.wait_ge(s["s_exp"], 16 * i + k + 1)
                        V_.reciprocal(ac[:, 3, k:k + 1], ac[:, 2, k:k + 1]).then_inc(s["rd_ready"], 1)
                        dve.wait_ge(s["rd_ready"], 16 * i + k + 1)
                        dve.wait_ge(s["pv_mm"], g0 + groups(h)[-1][0] + 3)
                        TS(ob[:, h, 64 * p:64 * p + 64], PS[:, 7, 0:64], ac[:, 3, k:k + 1], None, ALU.mult)\
                            .then_inc(s["ob_ready"], 1)

            turns(dve, turn)
            mix(TT - 1, 1)
            mix_low(TT - 1)
            end_phase(dve, 2)

            def residual(k, bank):
                TTo(x[:, k], x[:, k], acc(bank), ALU.add).then_inc(s["x_written"], 1)

            for n in range(8):
                prep(U_OUT1 + n + 2, (n + 2) % 4)
                dve.wait_ge(x_back[n // 4], 16)
                dve.wait_ge(s["w_used"], U_OUT1 + n + 1)
                residual(n, n % 2)
                add_square(1, n - 1)
            add_square(1, KT - 1)
            norm_factor(1)
            norm_halves(1, C_N2)

            F = U_FFN1

            def taps(dst, bank, col, tap0, conv, j):
                dve.wait_ge(s[tap0], j + 1)
                STT(dst[:, 1:S], acc(bank)[:, 0:S - 1], par[:, bass.ds(C_FF01 + 2 * FF1 + col, 1)], dst[:, 1:S],
                    ALU.mult, ALU.add).then_inc(s[conv], 1)
                dve.wait_ge(s[conv], 2 * j + 1)
                STT(dst[:, 2:S], acc(bank)[:, 0:S - 2], par[:, bass.ds(C_FF01 + col, 1)], dst[:, 2:S],
                    ALU.mult, ALU.add).then_inc(s[conv], 1)

            def inner(j, b):
                taps(uc, 1, j + FF1, "v_tap0", "v_conv", j)
                dve.wait_ge(s["v_conv"], 2 * j + 2)
                dve.wait_ge(s["f_silu"], j + 1)
                TTo(uc[:], gc[:], uc[:], ALU.mult).then_inc(s["a_f"], 1)
                low_a(j + 1, b)

            def low_a(count, b):
                dve.wait_ge(s["a_hi"], count)
                TTo(fl[:, b], uc[:], fh[:, b].bitcast(F32), ALU.subtract).then_inc(s["a_lo"], 1)

            def downs(j, m, i, unit, r=None):
                for t in range(KT):
                    if t < KT - 1:
                        dve.wait_ge(s["d_mm"], 7 * j + t + 1 + 7 * m * i)
                    else:
                        dve.wait_ge(s["w_used"], unit)
                    residual(t, 2 + t % 2)
                    if r is not None:
                        add_square(r, t - 1)
                if r is not None:
                    add_square(r, KT - 1)

            prep(F + 2, 2)
            taps(gc, 0, 0, "f_tap0", "f_conv", 0)
            prep(F + 3, 3)
            with dve.Fori(0, (FF1 - 2) // 2) as i:
                for u in range(2):
                    j = 2 * i + 1 + u
                    g = F + 2 + 3 * u
                    prep(g + 2, (g + 2 - F) % 6, 6, i)
                    inner(j - 1, u)
                    prep(g + 3, (g + 3 - F) % 6, 6, i)
                    taps(gc, 0, j, "f_tap0", "f_conv", j)
                    prep(g + 4, (g + 4 - F) % 6, 6, i)
                    downs(u, 2, i, g + 3 + 6 * i)
            g = U_IN2 - 4
            prep(g + 2, (g + 2 - F) % 6)
            inner(FF1 - 2, 0)
            prep(g + 3, (g + 3 - F) % 6)
            taps(gc, 0, FF1 - 1, "f_tap0", "f_conv", FF1 - 1)
            downs(FF1 - 2, 0, 0, g + 3)
            inner(FF1 - 1, 1)
            downs(FF1 - 1, 0, 0, g + 4, 2)
            prep(U_IN2, 0)
            norm_factor(2)
            norm_in_place(C_NF, 3)
            norm_factor(3)
            norm_halves(2, C_M1)
            prep(U_IN2 + 1, 1)

            V = U_IN2

            def gated(q):
                dve.wait_ge(s["g_sig"], q + 1)
                TTo(cg[:, q + 1], acc(2 * (q % 2)), sgb[:], ALU.mult).then_inc(s["g_ready"], 1)

            prep(V + 2, 2)
            prep(V + 3, 3)
            tap = 0
            for q in range(4):
                for d in range(TAPS31):
                    if tap % 16 == 0 and tap // 16 < 4:
                        gated(tap // 16)
                    if tap % 8 == 0 and tap // 8 < 12:
                        prep(V + 4 + tap // 8, (tap // 8) % 4)
                    w = par[:, C_C31 + 4 * (TAPS31 - 1 - d) + q:C_C31 + 4 * (TAPS31 - 1 - d) + q + 1]
                    if d == 0:
                        dve.wait_ge(s["g_ready"], q + 1)
                        done(TS(cg[:, q], cg[:, q + 1], w, par[:, C_CB + q:C_CB + q + 1], ALU.mult, ALU.add))
                    else:
                        done(STT(cg[:, q, d:S], cg[:, q + 1, 0:S - d], w, cg[:, q, d:S], ALU.mult, ALU.add))
                    tap += 1
            dve.wait_ge(s["v_gelu"], TT)
            TS(small[:, 40:48], small[:, 32:40], -1.0 / HALF, None, ALU.mult).then_inc(s["v_neg"], 1)
            dve.wait_ge(s["wt_mm"], 1)
            TTo(sgw[:, 1], heads(0), again(triu[:], GH), ALU.mult).then_inc(s["wt_ready"], 1)
            dve.wait_ge(s["v_ssq"], TT)
            TS(small[:, 56:64], small[:, 48:56], 1.0 / HALF, EPS, ALU.mult, ALU.add).then_inc(s["v_neg"], 1)
            dve.wait_ge(s["v_sd"], 1)
            done(V_.reciprocal(small[:, 72:80], small[:, 64:72]))
            for t in range(TT):
                TS(vt[:, t], vt[:, t], small[:, 40 + t:41 + t], small[:, 72 + t:73 + t], ALU.add, ALU.mult)\
                    .then_inc(s["v_n1"], 1)
            for t in range(TT + 1):
                if t < TT:
                    m = sgb[:, (t % 2) * HALF:(t % 2 + 1) * HALF].rearrange("p (h t) -> p h t", h=GH)
                    dve.wait_ge(s["m_mm"], TT + t + 1)
                    if t >= 2:
                        dve.wait_ge(s["m_lo"], t - 1)
                    TTo(m, heads(t % 4), bsb[:], ALU.add).then_inc(s["m_b"], 1)
                    dve.wait_ge(s["m_b"], t + 1)
                    TTo(m, m, ub[:, :, t * P:(t + 1) * P], ALU.mult).then_inc(s["m_u"], 1)
                if t:
                    q = t - 1
                    dve.wait_ge(s["m_hi"], t)
                    TTo(hl[:, 0:GH, q * P:(q + 1) * P],
                        sgb[:, (q % 2) * HALF:(q % 2 + 1) * HALF].rearrange("p (h t) -> p h t", h=GH),
                        hh[:, 0:GH, q * P:(q + 1) * P].bitcast(F32), ALU.subtract).then_inc(s["m_lo"], 1)
            for q in range(4):
                dve.wait_ge(s["lm_mm"], q + 1)
                STT(cg[:, q], acc(q), -1.0 / P, cg[:, q], ALU.mult, ALU.add).then_inc(s["lm_x"], 1)
            dve.wait_ge(s["lv_mm"], 1)
            TS(small[:, 96:128], PS[:, 0, 0:32], 1.0 / P, EPS, ALU.mult, ALU.add).then_inc(s["lv_v"], 1)
            dve.wait_ge(s["lv_sd"], 1)
            done(V_.reciprocal(small[:, 160:192], small[:, 128:160]))
            for q in range(4):
                TTo(vt[:, 2 * q:2 * q + 2].rearrange("p a (b n) -> p (a b) n", n=P), again(ident[:], TT),
                    first(small[:, 160 + 8 * q:168 + 8 * q], P), ALU.mult).then_inc(s["lv_d"], 1)
            for q in range(4):
                dve.wait_ge(s["lv_R"], q + 1)
                TTo(cg[:, q], cg[:, q], acc(q), ALU.mult).then_inc(s["lv_n"], 1)
            for q in range(4):
                dve.wait_ge(s["lv_h"], q + 1)
                TTo(hl[:, 4 + q], cg[:, q], hh[:, 4 + q].bitcast(F32), ALU.subtract).then_inc(s["lv_l"], 1)

            prep(U_OUT2, 0)
            prep(U_OUT2 + 1, 1)
            for n in range(8):
                prep(U_OUT2 + n + 2, (n + 2) % 4)
                dve.wait_ge(s["w_used"], U_OUT2 + n + 1)
                residual(n, n % 2)
                add_square(4, n - 1)
            add_square(4, KT - 1)
            norm_factor(4)
            norm_halves(3, C_M2)

            F = U_FFN2
            prep(F + 2, 2)
            with dve.Fori(0, (FF2 - 2) // 2) as i:
                for u in range(2):
                    up = F + 1 + 2 * u
                    low_a(FF1 + 1 + u + 2 * i, u)
                    prep(up + 2, (3 + 2 * u) % 4, 4, i)
                    downs(FF1 + u, 2, i, up + 2 + 4 * i)
                    prep(up + 3, (4 + 2 * u) % 4, 4, i)
            low_a(FF1 + FF2 - 1, 0)
            prep(U_END - 1, 3)
            downs(FF1 + FF2 - 2, 0, 0, U_END - 1)
            low_a(FF1 + FF2, 1)
            downs(FF1 + FF2 - 1, 0, 0, U_END, 5)
            norm_factor(5)
            norm_in_place(C_MF)

        @block.tensor
        def _(pe):
            mm, tr = nc.tensor.matmul, nc.tensor.transpose

            def unit(k, slot, bank, m=0, i=0, stats=None):
                pe.wait_ge(s["w_lo"], k + 1 + m * i)
                for kk in range(KT):
                    if stats is not None:
                        pe.wait_ge(s["n_lo"], KT * stats + kk + 1)
                    cut = slice(kk * P, kk * P + P)
                    for n, (w, h) in enumerate(((whs, hh), (whs, hl), (wls, hh))):
                        for t in range(2):
                            last = mm(acc(bank)[:, t * HALF:(t + 1) * HALF], w(slot)[:, cut],
                                      h[:, kk, t * HALF:(t + 1) * HALF], start=kk == 0 and n == 0,
                                      stop=kk == KT - 1 and n == 2)
                last.then_inc(s["w_used"], 1)

            def down(k, slot, b, count, xw, m=0, i=0):
                pe.wait_ge(s["w_lo"], k + 1 + m * i)
                pe.wait_ge(s["a_lo"], count)
                for t in range(KT):
                    pe.wait_ge(s["x_written"], xw + t - 1)
                    cut = slice(t * P, t * P + P)
                    for n, (w, h) in enumerate(((whs, fh), (whs, fl), (wls, fh))):
                        for q in range(2):
                            last = mm(acc(2 + t % 2)[:, q * HALF:(q + 1) * HALF], w(slot)[:, cut],
                                      h[:, b, q * HALF:(q + 1) * HALF], start=n == 0, stop=n == 2)
                    last.then_inc(s["d_mm" if t < KT - 1 else "w_used"], 1)

            def columns(src, dst, stop):
                for t in range(TT):
                    last = mm(dst(t), src[:, t * P:(t + 1) * P], ones[:, 0:1], start=True, stop=True)
                last.then_inc(*stop)

            def norm_factor(r):
                pe.wait_ge(s["n_acc"], 7 * r + 7)
                columns(nacc, lambda t: PS[:, 5, t:t + 1], (s["n_cols"], 1))
                pe.wait_ge(s["n_diag"], r + 1)
                for t in range(2):
                    last = mm(acc(3)[:, t * HALF:(t + 1) * HALF], ones[:], diag[:, 4 * t:4 * t + 4, :], start=True, stop=True)
                last.then_inc(s["n_R"], 1)

            def tokens(u, dst, free):
                pe.wait_ge(s["w_lo"], u + 4)
                for t in range(TT):
                    free(t)
                    for kk in range(KT):
                        cut = slice(kk * P, kk * P + P)
                        for n, (w, h) in enumerate(((wh, hh), (wl, hh), (wh, hl))):
                            last = mm(dst(t), h[:, kk, t * P:(t + 1) * P], w[:, :, cut], start=kk == 0 and n == 0,
                                      stop=kk == KT - 1 and n == 2)
                    yield last, t

            pe.wait_ge(s["const_loaded"], 32)
            pe.wait_ge(s["pack_loaded"], 16 * 14)
            for n, r in enumerate((109, 88, 44, 124)):
                last = tr(PS[:, 4, n * P:n * P + r], pack[0:r, n], ident[0:r, 0:r])
            last.then_inc(s["par_mm"], 1)
            pe.wait_ge(s["xin_loaded"], 16)
            for k in range(KT):
                if k >= 2:
                    pe.wait_ge(s["x_written"], k - 1)
                for t in range(TT):
                    last = tr(acc(k % 2)[:, t * P:(t + 1) * P], xin[:, t, k * P:(k + 1) * P], ident[:])
                last.then_inc(s["xt_mm"], 1)
            pe.wait_ge(s["consts_set"], 1)
            pe.wait_ge(s["x_written"], KT)
            pe.wait_ge(s["par_ready"], 4)
            norm_factor(0)
            for n in range(12):
                if n >= 2:
                    pe.wait_ge(s["st_written"], n - 1)
                unit(n, n % 4, n % 2, stats=0 if n == 0 else None)

            pe.wait_ge(s["sq_init"], 1)
            with pe.Fori(0, 3) as i:
                for u in range(4):
                    pe.wait_ge(s["st_written"], 11 + 4 * i + u)
                    unit(U_QKV + u, u, u % 2, 4, i)
                    pe.wait_ge(s["st_written"], 12 + 4 * i + u)
                    for tt in range(TT):
                        last = mm(PS[:, 7, bass.ds(tt * 12 + 4 * i + u, 1)], sqb[:, tt * P:(tt + 1) * P], ones[:, 0:1],
                                  start=True, stop=True)
                    last.then_inc(s["col_mm"], 1)

            for n in range(4):
                pe.wait_ge(s["st_written"], U_Z + n - 1)
                unit(U_Z + n, n, n % 2)
            pe.wait_ge(s["ba_lo"], 1)
            for t in range(TT):
                for kk in range(KT):
                    for n, (w, h) in enumerate(((bah, hh), (bal, hh), (bah, hl))):
                        last = mm(PS[:, 6, 8 * t:8 * t + 8], h[:, kk, t * P:(t + 1) * P], w[:, kk, :],
                                  start=kk == 0 and n == 0, stop=kk == KT - 1 and n == 2)
            end_phase(pe, 1)

            pe.wait_ge(s["tab_dve"], 3)
            mm(PS[:, 5, 0:32], triu[:], tab[:, :, T_G:T_G + 4], start=True, stop=True).then_inc(s["tab_mm"], 1)

            def four(bank, left, right, start=True, stop=True):
                for h in range(GH):
                    last = mm(heads(bank)[:, h], left[:, h], right[:, h], start=start, stop=stop)
                return last

            def turn_tiles(bank, src):
                for h in range(GH):
                    last = tr(heads(bank)[:, h], src[:, h], ident[:])
                return last

            def load(c, p, turns_before):
                pe.wait_ge(ch_loaded[p], 16 * (turns_before + 1))
                turn_tiles(1, ch[:, p, 4:8]).then_inc(s["kq_mm"], 1)
                pe.wait_ge(s["tri_ready"], 2 * c + 1)
                pe.wait_ge(s["s_ready"], c + 1)
                mm(PS[:, 0, :], ones[:], G["U"][:], start=True, stop=True).then_inc(s["gc_mm"], 1)

            def gram(c, p):
                turn_tiles(2, ch[:, p, 0:4]).then_inc(s["kq_mm"], 1)
                pe.wait_ge(s["d_raw"], c + 1)
                pe.wait_ge(s["gam_ready"], c + 1)
                turn_tiles(0, ch[:, p, 8:12]).then_inc(s["v_mm"], 1)

            def mix(c):
                pe.wait_ge(s["on_ready"], c + 1)
                pe.wait_ge(s["ob_ready"], 8 * c + 9)
                turn_tiles(7, G["oz"]).then_inc(s["ot_mm"], 1)

            pe.sem_inc(s["pv_mm"], 2)
            load(0, 0, 0)
            gram(0, 0)

            def turn(i, p, first_chunk, last_chunk):
                c = 2 * i + p
                g0 = 24 * i + 12 * p
                for stage in ORDER:
                    if stage == "values" and p == 0:
                        pe.wait_ge(pair_loaded, 16 * (i + 1))
                        pe.wait_ge(s["obl_ready"], i + 1)
                        for t in range(TT):
                            last = tr(PS[:, 3 + t // 4, (t % 4) * P:(t % 4 + 1) * P], qkvb[:, 2, t * P:(t + 1) * P], ident[:])
                        last.then_inc(s["vt_mm"], 1)
                    elif stage == "turn_back":
                        pe.wait_ge(s["kqn_ready"], 2 * c + 2)
                        turn_tiles(1, G["kn"]).then_inc(s["kqT_mm"], 1)
                        turn_tiles(2, G["qn"]).then_inc(s["kqT_mm"], 1)
                    elif stage == "pairs":
                        pe.wait_ge(s["kqT_ready"], 2 * c + 1)
                        four(1, G["knT"], G["knT"]).then_inc(s["gram_mm"], 1)
                        pe.wait_ge(s["kqT_ready"], 2 * c + 2)
                        four(2, G["knT"], G["qnT"]).then_inc(s["gram_mm"], 1)
                    elif stage == "invert":
                        pe.wait_ge(s["lat_ready"], 2 * c + 1)
                        pe.wait_ge(s["v_ready"], c + 1)
                        turn_tiles(0, G["LT"]).then_inc(s["l_mm"], 1)
                    elif stage[0] == "corner":
                        pe.wait_ge(s["lev_t"], 6 * c + stage[1])
                        four(0, G["LT"], G["T"]).then_inc(s["lev_l"], 1)
                    elif stage[0] == "join":
                        l = stage[1]
                        pe.wait_ge(s["lev_u"], 6 * c + l)
                        if l == 1:
                            pe.wait_ge(s["tt0_ready"], c + 1)
                            pe.wait_ge(s["lat_ready"], 2 * c + 2)
                        else:
                            pe.wait_ge(s["lev_tt"], 6 * c + l - 1)
                        if l < 6:
                            four(1, G["TT"], G["U"]).then_inc(s["lev_v"], 1)
                        four(2, G["U"], G["TT"]).then_inc(s["lev_w"], 1)
                    elif stage == "read":
                        pe.wait_ge(s["kqd_ready"], 2 * c + 1)
                        four(0, G["kd"], G["St"]).then_inc(s["ks_mm"], 1)
                    elif stage == "solve":
                        pe.wait_ge(s["r_ready"], c + 1)
                        pe.wait_ge(s["lev_tt"], 6 * c + 6)
                        four(1, G["TT"], G["v"]).then_inc(s["u_mm"], 1)
                    elif stage == "update":
                        pe.wait_ge(s["kqd_ready"], 2 * c + 2)
                        pe.wait_ge(s["u_ready"], c + 1)
                        pe.wait_ge(s["ke_ready"], c + 1)
                        for h in range(GH):
                            mm(heads(2)[:, h], G["qd"][:, h], G["St"][:, h], start=True, stop=False)
                            last = mm(heads(2)[:, h], G["AT"][:, h], G["u"][:, h], start=False, stop=True)
                        last.then_inc(s["os_mm"], 1)
                        four(0, G["ke"], G["u"]).then_inc(s["os_mm"], 1)
                    elif stage == "load" and not last_chunk:
                        load(c + 1, 1 - p, i + p)
                    elif stage == "heads" and p == 1:
                        pe.wait_ge(s["ob_ready"], 16 * (i + 1) + 1)
                        for t in range(TT):
                            last = tr(PS[:, 3 + t // 4, (t % 4) * P:(t % 4 + 1) * P], ob[:, t], ident[:])
                        last.then_inc(s["obt_mm"], 1)
                    elif stage == "gram" and not last_chunk:
                        pe.wait_ge(s["o_copied"], c + 1)
                        gram(c + 1, 1 - p)
                    elif stage == "mix" and not first_chunk:
                        mix(c - 1)
                    elif stage[0] == "scores" and stage[1] < 8:
                        h, n = stage[1], P * (stage[1] + 1)
                        pe.wait_ge(s["s_max"], 16 * i + 8 * p + h + 1)
                        if p == 0 and h == 0:
                            pe.wait_ge(s["vb_ready"], i + 1)
                        rows_ = slice(64 * p, 64 * p + 64)
                        for lo in range(0, n, HALF):
                            hi = min(n, lo + HALF)
                            last = mm(PS[:, 3 + lo // HALF, 0:hi - lo], qkvb[rows_, 0, h * P:h * P + P],
                                      qkvb[rows_, 1, lo:hi], start=True, stop=True)
                        last.then_inc(s["s_mm"], 1)
                    elif stage[0] == "weigh":
                        if stage[1] <= 8:
                            h = stage[1] - 1
                            pe.wait_ge(s["s_exp"], 16 * i + 8 * p + h + 1)
                            for g, n in groups(h):
                                pe.wait_ge(s["p_evac"], g0 + g + 1)
                                b0 = 4 * (g - groups(h)[0][0])
                                for b in range(n):
                                    last = tr(PS[:, 5 + g % 2, b * P:b * P + P],
                                              sm[:, h % 2, (b0 + b) * P:(b0 + b) * P + P], ident[:])
                                last.then_inc(s["p_mm"], 1)
                        if stage[1] >= 2:
                            h = stage[1] - 2
                            pe.wait_ge(s["ob_ready"], 16 * i + 8 * p + h + 1)
                            if h == 0 and not first_chunk:
                                pe.wait_ge(s["og_ready"], c)
                            for g, n in groups(h):
                                pe.wait_ge(s["p_evac"], g0 + g + 3)
                                b0 = 4 * (g - groups(h)[0][0])
                                for b in range(n):
                                    last = mm(PS[:, 7, 0:64], pt[:, g % 2, b * P:b * P + P],
                                              vb[:, b0 + b, 64 * p:64 * p + 64], start=b0 + b == 0, stop=b0 + b == h)
                                last.then_inc(s["pv_mm"], 1)

            turns(pe, turn)
            mix(TT - 1)
            end_phase(pe, 2)

            for n in range(8):
                if n >= 2:
                    pe.wait_ge(s["x_written"], X_OUT1 + n - 1)
                unit(U_OUT1 + n, n % 4, n % 2)
            norm_factor(1)

            F = U_FFN1
            unit(F, 0, 0, stats=1)
            unit(F + 1, 1, 1)
            with pe.Fori(0, (FF1 - 2) // 2) as i:
                for u in range(2):
                    j = 2 * i + 1 + u
                    g = F + 2 + 3 * u
                    pe.wait_ge(s["f_conv"], 2 * j)
                    unit(g, (g - F) % 6, 0, 6, i)
                    pe.wait_ge(s["v_conv"], 2 * j)
                    unit(g + 1, (g + 1 - F) % 6, 1, 6, i)
                    down(g + 2, (g + 2 - F) % 6, u, j, X_FFN1 + KT * (j - 1), 6, i)
            g, j = U_IN2 - 4, FF1 - 1
            pe.wait_ge(s["f_conv"], 2 * j)
            unit(g, (g - F) % 6, 0)
            pe.wait_ge(s["v_conv"], 2 * j)
            unit(g + 1, (g + 1 - F) % 6, 1)
            down(g + 2, (g + 2 - F) % 6, 0, j, X_FFN1 + KT * (j - 1))
            down(g + 3, (g + 3 - F) % 6, 1, j + 1, X_FFN1 + KT * j)
            norm_factor(2)
            norm_factor(3)

            V = U_IN2
            for n in range(8):
                if n >= 4:
                    pe.wait_ge(s["g_ready"], n // 2 - 1)
                unit(V + n, n % 4, n % 4, stats=2 if n == 0 else None)
            for h in range(GH):
                if h < 2:
                    pe.wait_ge(s["g_ready"], 3)
                else:
                    pe.wait_ge(s["u_gelu"], h - 1)
                unit(V + 8 + h, h % 4, h % 2)

            def v_free(t):
                pe.wait_ge(s["g_ready"], 4)
                if t >= 4:
                    pe.wait_ge(s["v_gelu"], t - 3)

            for last, t in tokens(V + 12, lambda t: PS[:, 4 + t % 4, :], v_free):
                last.then_inc(s["m_mm"], 1)
            pe.drain().then_inc(s["w_used"], 4)
            pe.wait_ge(s["sgu_loaded"], 64)
            pe.wait_ge(s["u_gelu"], GH)
            turn_tiles(0, sgw[:, 0]).then_inc(s["wt_mm"], 1)
            pe.wait_ge(s["wt_ready"], 1)
            for t in range(TT):
                pe.wait_ge(s["v_n2"], 2 * t + 2)
                if t >= 4:
                    pe.wait_ge(s["m_b"], t - 3)
                for h in range(GH):
                    last = mm(heads(t % 4)[:, h], vt[:, t, h * P:(h + 1) * P], sgw[:, 1, h], start=True, stop=True)
                last.then_inc(s["m_mm"], 1)
            pe.wait_ge(s["m_b"], TT)
            for q in range(4):
                for t in range(2):
                    last = mm(acc(q)[:, t * HALF:(t + 1) * HALF], ones[:], cg[:, q, t * HALF:(t + 1) * HALF],
                              start=True, stop=True)
                last.then_inc(s["lm_mm"], 1)
            pe.wait_ge(s["lm_x"], 4)
            for q in range(4):
                pe.wait_ge(s["lm_sq"], q + 1)
                for t in range(TT):
                    last = mm(PS[:, 0, 8 * q + t:8 * q + t + 1], ub[:, q, t * P:(t + 1) * P], ones[:, 0:1],
                              start=True, stop=True)
            last.then_inc(s["lv_mm"], 1)
            for q in range(4):
                pe.wait_ge(s["lv_d"], q + 1)
                for t in range(2):
                    last = mm(acc(q)[:, t * HALF:(t + 1) * HALF], ones[:], vt[:, 2 * q + t, :], start=True, stop=True)
                last.then_inc(s["lv_R"], 1)
            pe.wait_ge(s["m_lo"], TT)
            pe.wait_ge(s["lv_l"], 4)
            for n in range(8):
                if n >= 2:
                    pe.wait_ge(s["x_written"], X_OUT2 + n - 1)
                unit(U_OUT2 + n, n % 4, n % 2)
            norm_factor(4)

            F = U_FFN2
            unit(F, 0, 0, stats=3)
            with pe.Fori(0, (FF2 - 2) // 2) as i:
                for u in range(2):
                    j = 2 * i + 1 + u
                    up = F + 1 + 2 * u
                    pe.wait_ge(s["r_relu"], j)
                    unit(up, (1 + 2 * u) % 4, 1 - u, 4, i)
                    down(up + 1, (2 + 2 * u) % 4, u, FF1 + j, X_FFN2 + KT * (j - 1), 4, i)
            pe.wait_ge(s["r_relu"], FF2 - 1)
            unit(U_END - 3, 1, 1)
            down(U_END - 2, 2, 0, FF1 + FF2 - 1, X_END - 2 * KT)
            down(U_END - 1, 3, 1, FF1 + FF2, X_END - KT)
            norm_factor(5)
            pe.wait_ge(s["x_written"], X_END + KT)
            for t in range(TT):
                if t >= 4:
                    pe.wait_ge(s["fin_evac"], t - 3)
                for k in range(KT):
                    last = tr(acc(t % 4)[:, k * P:(k + 1) * P], x[:, k, t * P:(t + 1) * P], ident[:])
                last.then_inc(s["fin_mm"], 1)


def groups(h):
    if h < 4:
        return [(h, h + 1)]
    return [(2 * h - 4, 4), (2 * h - 3, h - 3)]


def shape_constants():
    at = np.arange(P)
    levels = [((at[:, None] // b) % 2 == 1) & (at[None, :] // b == at[:, None] // b - 1) for b in (1 << l for l in range(LEVELS))]
    dist = at[:, None] + (S - P) - np.arange(S)[None, :]
    held = sum(((dist >= 0) & (dist <= window) & (dist % step == 0)).astype(int) for window, step in ((128, 1), (512, 4), (2048, 16)))
    return {"c_ident": np.eye(P, dtype=np.float32),
            "c_triu": (at[:, None] <= at[None, :]).astype(np.float32),
            "c_levels": np.stack([levels[0].T] + levels, 1).astype(np.float32),
            "c_strip": np.where(held > 0, np.log(np.maximum(held, 1)), -1e30).astype(np.float32)}


def kernel(**inputs):
    import concourse.bacc as bacc
    from concourse.bass_utils import run_bass_kernel_spmd

    arrays = {name: np.ascontiguousarray(value) for name, value in {**inputs, **shape_constants()}.items()}
    nc = bacc.Bacc("TRN2", target_bir_lowering=False, num_devices=1)
    a = {name: nc.dram_tensor("in_" + name, v.shape, F32, kind="ExternalInput").ap() for name, v in arrays.items()}
    out = nc.dram_tensor("out", (1, S, D), F32, kind="ExternalOutput").ap()
    program(nc, a, out)
    r = run_bass_kernel_spmd(nc, [{"in_" + name: v for name, v in arrays.items()}], core_ids=[0])
    return r.results[0]["out"]
```

```python
from contextlib import ExitStack

import numpy as np

import concourse.bass as bass
from concourse import mybir

F32 = mybir.dt.float32
F32R = mybir.dt.float32r
ACT = mybir.ActivationFunctionType
ALU = mybir.AluOpType
AX_X = mybir.AxisListType.X

P = 128
D = 1024
S = 1024
KT = D // P
TT = S // P
HALF = 512
EPS = 1e-6
GH = 4
AH = 8
FF1 = 2816 // P
FF2 = 4096 // P
LEVELS = 7
TAPS31 = 31
LN0 = 2
CUT31 = 384

U_QKVB, U_QKV, U_Z, U_OUT1 = 0, 12, 24, 28
U_FFN1 = U_OUT1 + KT
U_IN2 = U_FFN1 + 3 * FF1
U_OUT2 = U_IN2 + 16
U_FFN2 = U_OUT2 + KT
U_END = U_FFN2 + 2 * FF2
X_OUT1 = KT
X_FFN1 = X_OUT1 + KT
X_MID = X_FFN1 + KT * FF1
X_OUT2 = X_MID + KT
X_FFN2 = X_OUT2 + KT
X_END = X_FFN2 + KT * FF2
C_N1, C_N2, C_NF, C_M1, C_M2, C_MF, C_CONV, C_CB, C_LG, C_LB = 0, 8, 16, 24, 32, 40, 48, 96, 100, 104
C_GN, C_FF01, C_FF2, C_C31 = 108, 128, 256, 384
T_RQ, T_RK, T_BETA, T_G, T_NGC, T_N = 0, 4, 8, 12, 16, 20


def first(ap, n):
    return ap.unsqueeze(2).broadcast_to([ap.shape[0], ap.shape[1], n])


def again(ap, n):
    return ap.unsqueeze(1).broadcast_to([ap.shape[0], n, ap.shape[1]])


def program(nc, a, out):
    ctx = ExitStack()
    with ctx:
        def dram(name, shape):
            return nc.dram_tensor(name, shape, F32, kind="Internal").ap()

        x_s, qkvz_s, qkvb_s = dram("x_s", [P, KT, S]), dram("qkvz_s", [P, 16, S]), dram("qkvb_s", [P, 12, S])

        def sb(name, shape, dt=F32, where=ctx):
            return where.enter_context(nc.sbuf_tensor(name, shape, dt))

        def sem(name):
            return ctx.enter_context(nc.semaphore(name))

        PS = ctx.enter_context(nc.psum_tensor("PS", [P, 8, HALF], F32))

        def acc(s):
            return PS[:, 2 * s:2 * s + 2, :].rearrange("p a b -> p (a b)")

        def heads(bank):
            return PS[:, bank, :].rearrange("p (h t) -> p h t", h=4)

        par = sb("par", [P, 512])
        ident = sb("ident", [P, P])
        triu = sb("triu", [P, P])
        ones = sb("ones", [P, P])
        small = sb("small", [P, 256])
        bah, bal, baw = sb("bah", [P, 8, 8], F32R), sb("bal", [P, 8, 8], F32R), sb("baw", [P, 8, 8])
        tab = small[:, 32:32 + TT * T_N].rearrange("p (t n) -> p t n", n=T_N)
        raw = sb("raw", [P, 2, D])
        wh, wl = sb("wh", [P, 4, D], F32R), sb("wl", [P, 4, D], F32R)
        hh, hl = sb("hh", [P, KT, S], F32R), sb("hl", [P, KT, S], F32R)

        with ExitStack() as z:
            strip, lmask = sb("strip", [P, S], where=z), sb("lmask", [P, LEVELS + 1, P], where=z)
            ch = sb("ch", [P, 2, 16, P], where=z)
            qkvb = sb("qkvb", [P, 3, S], where=z)
            vb = sb("vb", [P, TT, P], where=z)
            G = {n: sb(n, [P, GH, P], where=z) for n in
                 "bm E gam kn qn v knT qnT kd qd ke LT AT T TT U u St Sg oz".split()}
            G["og"] = G["u"]
            cc = sb("cc", [P, 2, T_N], where=z)
            oc = sb("oc", [P, 8, GH], where=z)
            sm = sb("sm", [P, 2, S], where=z)
            pt = sb("pt", [P, 2, HALF], where=z)
            ob = sb("ob", [P, TT, P], where=z)
            ac = sb("ac", [P, 4, 16], where=z)
        x = sb("x", [P, KT, S])
        with ExitStack() as z:
            xin = sb("xin", [P, TT, D], where=z)
            pack = sb("pack", [P, 4, P], where=z)
        with ExitStack() as z:
            st = sb("st", [P, 4, S], where=z)
            cacc = sb("cacc", [P, 2, S], where=z)
            sqb = sb("sqb", [P, S], where=z)
            tmpt = cacc[:, 0, 0:HALF].rearrange("p (a b) -> p a b", b=64)
        with ExitStack() as z:
            wh2, wl2 = sb("wh2", [P, 2, D], F32R, where=z), sb("wl2", [P, 2, D], F32R, where=z)
            fh, fl = sb("fh", [P, 2, S], F32R, where=z), sb("fl", [P, 2, S], F32R, where=z)
            gc = sb("gc", [P, S], where=z)
            uc = sb("uc", [P, S], where=z)
            nacc, sqt = sb("nacc", [P, S], where=z), sb("sqt", [P, 2, S], where=z)
            diag = sb("diag", [P, TT, P], where=z)
            hf = sb("hf", [P, 2, S], where=z)
        with ExitStack() as z:
            cg = sb("cg", [P, 5, S], where=z)
            sgb = sb("sgb", [P, S], where=z)
            sgw = sb("sgw", [P, 2, GH, P], where=z)
            bsb = sb("bsb", [P, GH, P], where=z)
            lng, lnb = sb("lng", [P, HALF], where=z), sb("lnb", [P, HALF], where=z)
            vt = sb("vt", [P, TT, HALF], where=z)
            ub = sb("ub", [P, GH, S], where=z)

        def whs(slot):
            return (wh[:, slot] if slot < 4 else wh2[:, slot - 4])

        def wls(slot):
            return (wl[:, slot] if slot < 4 else wl2[:, slot - 4])

        def out_tile(t):
            return (hf[:, 0], hf[:, 1], gc[:], uc[:])[t % 4]

        def out_acc(t):
            return acc((0, 1, 3)[t % 3])

        def tap31(q, d):
            at = C_C31 + 4 * (TAPS31 - 1 - d) + q
            return par[:, at:at + 1]

        def mixed(t):
            return sgb[:, (t % 2) * HALF:(t % 2 + 1) * HALF].rearrange("p (h t) -> p h t", h=GH)

        def spread(q):
            return (cg[:, 4] if q % 2 == 0 else sgb[:]).rearrange("p (a n) -> p a n", n=P)

        names = """const_loaded rows_loaded pack_loaded par_mm par_ready consts_set xin_loaded xt_mm x_written x_spilled
            w_hi w_lo w_used n_sq n_acc n_cols n_v n_sd n_diag n_R n_x n_hi n_lo v_chain tap0 conv silu sq_init
            col_mm ba_loaded ba_hi ba_lo ba_mm ba_copied st_written phase_end tab_dve tab_act tab_mm tables_loaded
            cc_ready tri_ready gc_mm kq_mm gam_ready d_ready e_ready vt_mm vb_ready tt0_ready o_copied og_ready
            kqn_ready v_mm v_ready kqT_mm kqT_ready eb_ready gram_mm lat_ready kqd_ready ke_ready sg_ready l_mm
            u0_ready lev_l lev_u lev_v lev_w lev_t lev_tt ks_mm r_ready u_mm u_ready s_ready os_mm osq o_v o_sd o_r
            on_ready ot_mm oh_ready ol_ready s_mm s_max s_neg s_exp p_mm p_evac pv_mm rd_ready ob_ready obt_mm
            obh_ready obl_ready f_tap0 f_conv f_silu v_tap0 v_conv a_f a_hi a_lo d_mm g_sig g_ready u_gelu v_gelu
            v_neg v_ssq v_sd v_var v_n1 v_n2 wt_mm c_dve prod_ready p_chain wt_ready m_mm m_b m_u m_hi m_lo lm_mm
            lm_x lm_sq lv_mm lv_v lv_sd lv_d lv_R lv_n lv_h lv_l r_relu r_sq fin_mm fin_evac sgu_loaded""".split()
        s = {n: sem(n) for n in names}

        w_loaded = [sem(f"w_loaded{i}") for i in range(2)]
        st_free = [sem(f"st_free{i}") for i in range(4)]
        ch_loaded = [sem(f"ch_loaded{i}") for i in range(2)]
        pair_loaded = sem("pair_loaded")
        x_back = [sem(f"x_back{i}") for i in range(2)]
        out_stored = [sem(f"out_stored{i}") for i in range(4)]

        def end_phase(eng, n):
            eng.drain().then_inc(s["phase_end"], 1)
            eng.wait_ge(s["phase_end"], 5 * n)

        w_in, w_out, w_up, w_down = a["w_in"][0], a["w_out"][0], a["w_up"][0], a["w_down"][0]
        w_in2, w_out2, w_ff1, w_ff2 = a["w_in_2"][0], a["w_out_2"][0], a["w_ff1_2"][0], a["w_ff2_2"][0]

        def cols(w, c):
            return w.rearrange("(k p) n -> p k n", p=P)[:, :, bass.ds(c, P)]

        def rows(w, r):
            return w[bass.ds(r, P), :]

        ORDER = ["values", "turn_back", ("scores", 0), "pairs", "mix", "invert", ("scores", 1), ("weigh", 1)]
        for l in range(1, LEVELS):
            ORDER += [("corner", l), ("scores", l + 1), ("join", l), ("weigh", l + 1)]
        ORDER += ["begin", "read", ("weigh", 8), "solve", ("weigh", 9), "update", "load", "heads", "gram", "root"]

        def turns(eng, turn):
            for p in range(2):
                turn(0, p, p == 0, False)
            with eng.Fori(1, TT // 2 - 1) as i:
                for p in range(2):
                    turn(i, p, False, False)
            for p in range(2):
                turn(TT // 2 - 1, p, False, p == 1)

        block = ctx.enter_context(nc.Block())

        @block.sync
        def _(sp):
            def load(k, src, m=0, i=0, down=False):
                if k >= 2:
                    sp.wait_ge(s["w_lo"], k - 1 + m * i)
                dst = raw[:, k % 2] if down else raw[:, k % 2].rearrange("p (k n) -> p k n", k=KT)
                sp.dma_start(dst, src).then_inc(w_loaded[k % 2], 16)

            sp.dma_start(xin[:], a["x"][0].rearrange("(t p) d -> p t d", p=P)).then_inc(s["xin_loaded"], 16)
            for dst, src in ((ident, a["c_ident"]), (triu, a["c_triu"])):
                sp.dma_start(dst[:], src).then_inc(s["const_loaded"], 16)
            n = 0
            for name, lo in (("norm1_w", C_N1), ("norm2_w", C_N2), ("final_norm_w", C_NF), ("norm1_g_2", C_M1),
                             ("norm2_g_2", C_M2), ("final_g_2", C_MF)):
                v = a[name] if len(a[name].shape) == 1 else a[name][0]
                sp.dma_start(pack[lo:lo + 8, 0], v.rearrange("(r p) -> r p", p=P)).then_inc(s["pack_loaded"], 16)
            sp.dma_start(pack[C_CONV:C_CONV + 48, 0],
                         a["conv_qkv_w"][0].rearrange("a (r p) -> (a r) p", p=P)).then_inc(s["pack_loaded"], 16)
            for name, lo in (("conv_b_2", C_CB), ("conv_ln_g_2", C_LG), ("conv_ln_b_2", C_LB)):
                sp.dma_start(pack[lo:lo + 4, 0], a[name][0].rearrange("(r p) -> r p", p=P)).then_inc(s["pack_loaded"], 16)
            sp.dma_start(pack[C_GN:C_GN + 1, 0], a["gdn_norm_w"]).then_inc(s["pack_loaded"], 16)
            ff = a["ffn_conv_w"][0].rearrange("a (r p) -> (a r) p", p=P)
            sp.dma_start(pack[0:88, 1], ff[0:88, :]).then_inc(s["pack_loaded"], 16)
            sp.dma_start(pack[0:44, 2], ff[88:132, :]).then_inc(s["pack_loaded"], 16)
            sp.dma_start(pack[0:124, 3], a["conv_w_2"][0].rearrange("a (r p) -> (a r) p", p=P)).then_inc(s["pack_loaded"], 16)
            for dst, src in ((small[:, 0:4], a["dt_bias"][0]), (small[:, 4:8], a["a_log"][0])):
                sp.dma_start(dst, src.partition_broadcast(P)).then_inc(s["rows_loaded"], 16)
            sp.dma_start(baw[:], w_in.rearrange("(k p) n -> p k n", p=P)[:, :, 2048:2056]).then_inc(s["ba_loaded"], 16)

            for n in range(12):
                load(U_QKVB + n, cols(w_in, 2056 + P * n))
            with sp.Fori(0, 3) as i:
                for u in range(4):
                    load(U_QKV + u, cols(w_in, (4 * i + u) * P), 4, i)
            for n in range(4):
                load(U_Z + n, cols(w_in, 1536 + P * n))
            for n in range(2):
                load(U_OUT1 + n, cols(w_out, P * n))
            end_phase(sp, 1)


            def chunk(c):
                sp.dma_start(ch[:, c % 2], qkvz_s[:, :, c * P:(c + 1) * P]).then_inc(ch_loaded[c % 2], 16)

            def pair(t):
                sp.dma_start(qkvb[:], qkvb_s.rearrange("p (m t) s -> p m t s", m=3)[:, :, t, :]).then_inc(pair_loaded, 16)

            chunk(0)
            pair(0)
            sp.dma_start(strip[:], a["c_strip"]).then_inc(s["tables_loaded"], 16)
            sp.dma_start(lmask[:], a["c_levels"]).then_inc(s["tables_loaded"], 16)
            chunk(1)
            for i in range(1, 4):
                sp.wait_ge(s["og_ready"], 2 * i - 1)
                chunk(2 * i)
                sp.wait_ge(s["s_mm"], 16 * i)
                pair(i)
                sp.wait_ge(s["og_ready"], 2 * i)
                chunk(2 * i + 1)
            end_phase(sp, 2)

            for m in range(2):
                sp.dma_start(x[:, 4 * m:4 * m + 4], x_s[:, 4 * m:4 * m + 4]).then_inc(x_back[m], 16)
            for n in range(2, 4):
                load(U_OUT1 + n, cols(w_out, P * n))
            for n in range(4, 8):
                load(U_OUT1 + n, cols(w_out, P * n))

            F = U_FFN1
            load(F, cols(w_up, 0))
            load(F + 1, cols(w_up, FF1 * P))
            with sp.Fori(0, (FF1 - 2) // 2) as i:
                for u in range(2):
                    j = 2 * i + 1 + u
                    load(F + 2 + 3 * u, cols(w_up, j * P), 6, i)
                    load(F + 3 + 3 * u, cols(w_up, (j + FF1) * P), 6, i)
                    load(F + 4 + 3 * u, rows(w_down, (j - 1) * P), 6, i, down=True)
            load(U_IN2 - 4, cols(w_up, (FF1 - 1) * P))
            load(U_IN2 - 3, cols(w_up, (2 * FF1 - 1) * P))
            load(U_IN2 - 2, rows(w_down, (FF1 - 2) * P), down=True)
            load(U_IN2 - 1, rows(w_down, (FF1 - 1) * P), down=True)

            with sp.Fori(0, 2) as i:
                for u in range(4):
                    load(U_IN2 + u, cols(w_in2, 1024 + 512 * (u % 2) + (2 * i + u // 2) * P), 4, i)
            for n in range(4):
                load(U_IN2 + 8 + n, cols(w_in2, P * n))
            for n in range(4):
                load(U_IN2 + 12 + n, cols(w_in2, 512 + P * n))
            sp.wait_ge(s["g_ready"], 1)
            sp.dma_start(bsb[:], a["sgu_b_2"][0].partition_broadcast(P)).then_inc(s["sgu_loaded"], 16)
            sp.dma_start(lng[:], a["sgu_ln_g_2"][0].partition_broadcast(P)).then_inc(s["sgu_loaded"], 16)
            sp.dma_start(lnb[:], a["sgu_ln_b_2"][0].partition_broadcast(P)).then_inc(s["sgu_loaded"], 16)
            sp.dma_start(sgw[:, 0], a["sgu_w_2"][0].rearrange("h t s -> t h s")).then_inc(s["sgu_loaded"], 16)
            for n in range(8):
                load(U_OUT2 + n, cols(w_out2, P * n))
            F = U_FFN2
            load(F, cols(w_ff1, 0))
            with sp.Fori(0, (FF2 - 2) // 2) as i:
                for u in range(2):
                    j = 2 * i + 1 + u
                    load(F + 1 + 2 * u, cols(w_ff1, j * P), 4, i)
                    load(F + 2 + 2 * u, rows(w_ff2, (j - 1) * P), 4, i, down=True)
            load(U_END - 3, cols(w_ff1, (FF2 - 1) * P))
            load(U_END - 2, rows(w_ff2, (FF2 - 2) * P), down=True)
            load(U_END - 1, rows(w_ff2, (FF2 - 1) * P), down=True)

            sp.wait_ge(s["w_lo"], U_END - 1)
            sp.dma_start(raw[:, 0], a["final_g_2"].partition_broadcast(P)).then_inc(s["tables_loaded"], 16)
            for t in range(TT):
                sp.wait_ge(s["fin_evac"], t + 1)
                sp.dma_start(out[0, t * P:(t + 1) * P, :], out_tile(t)).then_inc(out_stored[t % 4], 16)
            for b in range(4):
                sp.wait_ge(out_stored[b], 16 * (TT // 4))

        @block.gpsimd
        def _(pool):
            nc.gpsimd.memset(ones[:], 1.0).then_inc(s["consts_set"], 1)
            pool.wait_ge(s["const_loaded"], 32)
            pool.wait_ge(s["x_written"], KT)
            pool.dma_start(x_s, x[:]).then_inc(s["x_spilled"], 16)
            for n in range(12):
                pool.wait_ge(s["st_written"], n + 1)
                pool.dma_start(qkvb_s[:, n], st[:, n % 4]).then_inc(st_free[n % 4], 16)
            with pool.Fori(0, 3) as i:
                for u in range(4):
                    pool.wait_ge(s["st_written"], 13 + u + 4 * i)
                    pool.dma_start(qkvz_s[:, bass.ds(4 * i + u, 1), :], st[:, u:u + 1]).then_inc(st_free[u], 16)
            for n in range(4):
                pool.wait_ge(s["st_written"], U_Z + n + 1)
                pool.dma_start(qkvz_s[:, 12 + n], st[:, n]).then_inc(st_free[n], 16)
            for b in range(4):
                pool.wait_ge(st_free[b], 16 * 7)
            pool.wait_ge(s["x_spilled"], 16)
            end_phase(pool, 1)

            PT = nc.gpsimd.tensor_tensor
            nc.gpsimd.memset(G["St"][:], 0.0).then_inc(s["s_ready"], 1)

            def begin(c, p):
                cp = cc[:, p]
                pool.wait_ge(s["cc_ready"], c + 1)
                PT(G["U"][:], again(triu[:], GH), first(cp[:, T_G:T_G + 4], P), ALU.mult).then_inc(s["tri_ready"], 1)
                PT(G["bm"][:], again(triu[:], GH), first(cp[:, T_BETA:T_BETA + 4], P), ALU.mult).then_inc(s["tri_ready"], 1)

            begin(0, 0)

            def turn(i, p, first_chunk, last):
                c = 2 * i + p
                for stage in ORDER:
                    if stage == "invert":
                        pool.wait_ge(s["lat_ready"], 2 * c + 1)
                        PT(G["TT"][:], G["LT"][:], again(lmask[:, 0], GH), ALU.mult).then_inc(s["tt0_ready"], 1)
                        pool.wait_ge(s["tt0_ready"], 2 * c + 1)
                        PT(G["TT"][:], again(ident[:], GH), G["TT"][:], ALU.subtract).then_inc(s["tt0_ready"], 1)
                        pool.wait_ge(s["gam_ready"], c + 1)
                        pool.wait_ge(s["kqT_ready"], 2 * c + 2)
                        PT(G["kd"][:], G["knT"][:], G["gam"][:], ALU.mult).then_inc(s["kqd_ready"], 1)
                        PT(G["qd"][:], G["qnT"][:], G["gam"][:], ALU.mult).then_inc(s["kqd_ready"], 1)
                        pool.wait_ge(s["eb_ready"], c + 1)
                        PT(G["ke"][:], G["kn"][:], G["E"][:, :, P - 1:P].broadcast_to([P, GH, P]), ALU.mult)\
                            .then_inc(s["ke_ready"], 1)
                        pool.wait_ge(s["s_ready"], c + 1)
                        PT(G["Sg"][:], G["St"][:], G["gam"][:, :, P - 1:P].broadcast_to([P, GH, P]), ALU.mult)\
                            .then_inc(s["sg_ready"], 1)
                    elif stage == "begin" and not last:
                        pool.wait_ge(s["lev_w"], 6 * c + 6)
                        begin(c + 1, 1 - p)
                    elif stage == "root":
                        pool.wait_ge(s["o_copied"], c + 1)
                        pool.wait_ge(s["o_r"], c + 1)
                        PT(G["oz"][:], G["oz"][:], first(oc[:, 3], P), ALU.mult).then_inc(s["on_ready"], 1)

            turns(pool, turn)
            end_phase(pool, 2)

            for step in range(4 * TAPS31):
                q, d = divmod(step, TAPS31)
                if d == 0:
                    pool.wait_ge(s["g_ready"], q + 1)
                    if q:
                        pool.wait_ge(s["c_dve"], q)
                    nc.gpsimd.tensor_scalar(cg[:, q, 0:CUT31], cg[:, q + 1, 0:CUT31], tap31(q, 0),
                                            par[:, C_CB + q:C_CB + q + 1], ALU.mult, ALU.add).then_inc(s["p_chain"], 1)
                else:
                    pool.wait_ge(s["prod_ready"], step - q)
                    pool.wait_ge(s["p_chain"], step)
                    nc.gpsimd.tensor_tensor(cg[:, q, d:CUT31], cg[:, q, d:CUT31], vt[:, 6 + step % 2, 0:CUT31 - d],
                                            ALU.add).then_inc(s["p_chain"], 1)
            for t in range(TT):
                pool.wait_ge(s["m_b"], t + 1)
                nc.gpsimd.tensor_tensor(mixed(t), mixed(t), ub[:, :, t * P:(t + 1) * P], ALU.mult).then_inc(s["m_u"], 1)

        @block.scalar
        def _(act):
            A = nc.scalar.activation

            def prep(k, slot, m=0, i=0):
                act.wait_ge(w_loaded[k % 2], 16 * (k // 2 + 1) + 8 * m * i)
                if k >= 4:
                    act.wait_ge(s["w_used"], k - 3 + m * i)
                A(whs(slot), raw[:, k % 2], ACT.Copy).then_inc(s["w_hi"], 1)

            def square(r, k, xbase):
                act.wait_ge(s["x_written"], xbase + k + 1)
                if k >= 3:
                    act.wait_ge(s["n_acc"], 7 * r + k - 2)
                A(sqt[:, k % 2] if k else nacc[:], x[:, k], ACT.Square).then_inc(s["n_sq"], 1)

            def norm_root(r):
                act.wait_ge(s["n_v"], r + 1)
                A(small[:, 16:24], small[:, 8:16], ACT.Sqrt).then_inc(s["n_sd"], 1)

            def norm_stats(r, xbase):
                for k in range(KT):
                    square(r, k, xbase)
                norm_root(r)

            def norm_halves(q):
                for k in range(KT):
                    act.wait_ge(s["n_x"], KT * q + k + 1)
                    A(hh[:, k], hf[:, k % 2], ACT.Copy).then_inc(s["n_hi"], 1)

            prep(0, 0)
            norm_stats(0, 0)
            norm_halves(0)
            prep(1, 1)
            act.wait_ge(s["ba_loaded"], 16)
            A(bah[:], baw[:], ACT.Copy).then_inc(s["ba_hi"], 1)

            for n in range(12):
                prep(n + 2, (n + 2) % 4)
                act.wait_ge(s["w_used"], n + 1)
                if n >= 4:
                    act.wait_ge(st_free[n % 4], 16 * (n // 4))
                A(st[:, n % 4], acc(n % 2), ACT.Copy, scale=(0.125 if n < 4 else 1.0)).then_inc(s["st_written"], 1)
            act.wait_ge(s["st_written"], 12)
            A(sqb[:], st[:, 3], ACT.Square).then_inc(s["sq_init"], 1)
            with act.Fori(0, 3) as i:
                for u in range(4):
                    prep(U_QKV + u + 2, (u + 2) % 4, 4, i)
                    act.wait_ge(s["w_used"], U_QKV + u + 1 + 4 * i)
                    A(cacc[:, u % 2], acc(u % 2), ACT.Copy,
                      scale=par[:, bass.ds(C_CONV + 36 + 4 * i + u, 1)]).then_inc(s["tap0"], 1)
                    act.wait_ge(s["conv"], 12 * i + 3 * u + 3)
                    act.wait_ge(st_free[u], 48 + 16 * i)
                    A(st[:, u], cacc[:, u % 2], ACT.Silu).then_inc(s["silu"], 1)
                    act.wait_ge(s["silu"], 4 * i + u + 1)
                    act.wait_ge(s["col_mm"], 4 * i + u + 1)
                    A(sqb[:], st[:, u], ACT.Square).then_inc(s["st_written"], 1)
            act.wait_ge(s["ba_mm"], 1)
            A(cacc[0:8, 1, :], acc(2)[0:8], ACT.Copy).then_inc(s["ba_copied"], 1)
            for n in range(4):
                prep(U_Z + n + 2, (n + 2) % 4)
                act.wait_ge(s["w_used"], U_Z + n + 1)
                act.wait_ge(st_free[n], 96)
                A(st[:, n], acc(n % 2), ACT.Silu).then_inc(s["st_written"], 1)
                if n == 0:
                    act.wait_ge(s["rows_loaded"], 32)
                    act.wait_ge(s["tab_dve"], 1)
                    A(tmpt[:, 1], tmpt[:, 0], ACT.Sqrt).then_inc(s["tab_act"], 1)
                    act.wait_ge(s["tab_dve"], 2)
                    A(tmpt[:, 3, 0:32], tmpt[:, 2, 0:32], ACT.Sigmoid).then_inc(s["tab_act"], 1)
                    A(tmpt[:, 5, 0:32], tmpt[:, 4, 32:64], ACT.Exp, scale=-1.0).then_inc(s["tab_act"], 1)
                    A(small[:, 24:28], small[:, 4:8], ACT.Exp).then_inc(s["tab_act"], 1)
            end_phase(act, 1)


            def load(c):
                act.wait_ge(s["gc_mm"], c + 1)
                A(G["gam"][:], heads(0), ACT.Exp).then_inc(s["gam_ready"], 1)

            def gram(c):
                act.wait_ge(s["d_ready"], 2 * c + 2)
                A(G["E"][:], G["E"][:], ACT.Exp).then_inc(s["e_ready"], 1)
                act.wait_ge(s["v_mm"], c + 1)
                A(G["v"][:], heads(0), ACT.Copy).then_inc(s["v_ready"], 1)

            def mix(c):
                act.wait_ge(s["og_ready"], c + 1)
                A(hh[:, 0:GH, bass.ds(c * P, P)], G["og"][:], ACT.Copy).then_inc(s["oh_ready"], 1)

            act.sem_inc(s["p_evac"], 2)
            load(0)
            gram(0)

            def turn(i, p, first_chunk, last):
                c = 2 * i + p
                g0 = 24 * i + 12 * p
                for stage in ORDER:
                    if stage == "values" and p == 0:
                        act.wait_ge(s["vt_mm"], i + 1)
                        A(vb[:].rearrange("p t d -> p (t d)"), PS[:, 3:5, :].rearrange("p a b -> p (a b)"), ACT.Copy)\
                            .then_inc(s["vb_ready"], 1)
                    elif stage == "turn_back":
                        act.wait_ge(s["kqT_mm"], 2 * c + 1)
                        A(G["knT"][:], heads(1), ACT.Copy).then_inc(s["kqT_ready"], 1)
                        act.wait_ge(s["kqT_mm"], 2 * c + 2)
                        A(G["qnT"][:], heads(2), ACT.Copy).then_inc(s["kqT_ready"], 1)
                    elif stage == "solve":
                        act.wait_ge(s["u_mm"], c + 1)
                        A(G["u"][:], heads(1), ACT.Copy).then_inc(s["u_ready"], 1)
                    elif stage == "update":
                        act.wait_ge(s["os_mm"], 2 * c + 1)
                        A(G["oz"][:], heads(2), ACT.Copy).then_inc(s["o_copied"], 1)
                        act.wait_ge(s["o_copied"], c + 1)
                        A(G["v"][:], G["oz"][:], ACT.Square).then_inc(s["osq"], 1)
                    elif stage == "load" and not last:
                        load(c + 1)
                    elif stage == "heads" and p == 1:
                        act.wait_ge(s["obt_mm"], i + 1)
                        A(hh[:, bass.ds(4 + i, 1), :].rearrange("p a s -> p (a s)"),
                          PS[:, 3:5, :].rearrange("p a b -> p (a b)"), ACT.Copy).then_inc(s["obh_ready"], 1)
                    elif stage == "gram" and not last:
                        act.wait_ge(s["o_v"], 2 * c + 1)
                        gram(c + 1)
                    elif stage == "root":
                        act.wait_ge(s["o_v"], 2 * c + 2)
                        A(oc[:, 2], oc[:, 1], ACT.Sqrt).then_inc(s["o_sd"], 1)
                    elif stage == "mix" and not first_chunk:
                        mix(c - 1)
                    elif stage[0] == "scores" and stage[1] < 8:
                        h, n = stage[1], P * (stage[1] + 1)
                        act.wait_ge(s["s_neg"], 16 * i + 8 * p + h + 1)
                        A(sm[:, h % 2, 0:n], sm[:, h % 2, 0:n], ACT.Exp, bias=ac[:, 1, 8 * p + h:8 * p + h + 1],
                          accum_out=ac[:, 2, 8 * p + h:8 * p + h + 1]).then_inc(s["s_exp"], 1)
                    elif stage[0] == "weigh" and stage[1] <= 8:
                        for g, n in groups(stage[1] - 1):
                            act.wait_ge(s["p_mm"], g0 + g + 1)
                            act.wait_ge(s["pv_mm"], g0 + g + 1)
                            A(pt[:, g % 2, 0:n * P], PS[:, 5 + g % 2, 0:n * P], ACT.Copy).then_inc(s["p_evac"], 1)

            turns(act, turn)
            mix(TT - 1)
            end_phase(act, 2)

            for n in range(8):
                prep(U_OUT1 + n + 2, (n + 2) % 4)
                if n:
                    square(1, n - 1, X_OUT1)
            square(1, KT - 1, X_OUT1)
            norm_root(1)
            norm_halves(1)

            F = U_FFN1

            def last_tap(dst, col, name, k, bank, m=0, i=0):
                act.wait_ge(s["w_used"], k + 1 + m * i)
                A(dst[:], acc(bank), ACT.Copy, scale=par[:, bass.ds(col, 1)]).then_inc(s[name], 1)

            def gate_silu(j):
                act.wait_ge(s["f_conv"], 2 * j + 2)
                A(gc[:], gc[:], ACT.Silu).then_inc(s["f_silu"], 1)

            def high_a(count, b, used):
                act.wait_ge(s["a_f"], count)
                act.wait_ge(s["w_used"], used)
                A(fh[:, b], uc[:], ACT.Copy).then_inc(s["a_hi"], 1)

            prep(F + 2, 2)
            last_tap(gc, C_FF2, "f_tap0", F, 0)
            prep(F + 3, 3)
            gate_silu(0)
            with act.Fori(0, (FF1 - 2) // 2) as i:
                for u in range(2):
                    j = 2 * i + 1 + u
                    g = F + 2 + 3 * u
                    prep(g + 2, (g + 2 - F) % 6, 6, i)
                    last_tap(uc, C_FF2 + FF1 - 1 + j, "v_tap0", g - 2 if u else F + 1, 1, 6, i)
                    high_a(j, u, g - 3 + 6 * i)
                    prep(g + 3, (g + 3 - F) % 6, 6, i)
                    last_tap(gc, C_FF2 + j, "f_tap0", g, 0, 6, i)
                    gate_silu(j)
                    prep(g + 4, (g + 4 - F) % 6, 6, i)
            g = U_IN2 - 4
            prep(g + 2, (g + 2 - F) % 6)
            last_tap(uc, C_FF2 + 2 * FF1 - 2, "v_tap0", g - 2, 1)
            high_a(FF1 - 1, 0, g - 3)
            prep(g + 3, (g + 3 - F) % 6)
            last_tap(gc, C_FF2 + FF1 - 1, "f_tap0", g, 0)
            gate_silu(FF1 - 1)
            last_tap(uc, C_FF2 + 2 * FF1 - 1, "v_tap0", g + 1, 1)
            high_a(FF1, 1, g)
            prep(U_IN2, 0)
            norm_stats(2, X_FFN1 + KT * (FF1 - 1))
            norm_stats(3, X_MID)
            norm_halves(2)
            prep(U_IN2 + 1, 1)

            V = U_IN2
            prep(V + 2, 2)
            prep(V + 3, 3)
            for step in range(4 * TAPS31):
                q, d = divmod(step, TAPS31)
                if step % 21 == 0 and step // 21 < 4:
                    g = step // 21
                    act.wait_ge(s["w_used"], V + 2 * g + 2)
                    if g:
                        act.wait_ge(s["g_ready"], g)
                    A(sgb[:], acc(2 * (g % 2) + 1), ACT.Sigmoid).then_inc(s["g_sig"], 1)
                if step % 9 == 3 and step // 9 < 12:
                    prep(V + 4 + step // 9, (step // 9) % 4)
                if step in (72, 82, 92, 103):
                    h = (step - 72) // 10
                    act.wait_ge(s["w_used"], V + 9 + h)
                    A(ub[:, h], acc(h % 2), ACT.Gelu).then_inc(s["u_gelu"], 1)
                if d:
                    act.wait_ge(s["g_ready"], q + 1)
                    if step >= 2:
                        act.wait_ge(s["p_chain"], step - 1)
                    A(vt[:, 6 + step % 2, 0:CUT31 - d], cg[:, q + 1, 0:CUT31 - d], ACT.Copy, scale=tap31(q, d))\
                        .then_inc(s["prod_ready"], 1)

            def value_squares(t):
                act.wait_ge(s["v_neg"], t + 1)
                A(PS[:, 4 + t % 4, :], vt[:, t], ACT.Square, bias=small[:, 40 + t:41 + t],
                  accum_out=small[:, 48 + t:49 + t]).then_inc(s["v_ssq"], 1)

            for t in range(TT):
                if 0 <= t - LN0 - 1 < 4:
                    q = t - LN0 - 1
                    act.wait_ge(s["lm_x"], q + 1)
                    if q:
                        act.wait_ge(s["lv_mm"], q)
                    A(sgb[:], cg[:, q], ACT.Square).then_inc(s["lm_sq"], 1)
                if t == LN0 + 5:
                    act.wait_ge(s["lv_v"], 4)
                    A(small[:, 128:160], small[:, 96:128], ACT.Sqrt).then_inc(s["lv_sd"], 1)
                act.wait_ge(s["m_mm"], t + 1)
                if t == 6:
                    act.wait_ge(s["p_chain"], 4 * TAPS31)
                A(vt[:, t], PS[:, 4 + t % 4, :], ACT.Gelu, accum_out=small[:, 32 + t:33 + t]).then_inc(s["v_gelu"], 1)
                if t:
                    value_squares(t - 1)
            value_squares(TT - 1)
            act.wait_ge(s["v_var"], 1)
            A(small[:, 64:72], small[:, 56:64], ACT.Sqrt).then_inc(s["v_sd"], 1)
            for q in range(4):
                act.wait_ge(s["lv_n"], q + 1)
                A(cg[:, q], cg[:, q], ACT.Silu, scale=par[:, C_LG + q:C_LG + q + 1],
                  bias=par[:, C_LB + q:C_LB + q + 1]).then_inc(s["lv_h"], 1)
                act.wait_ge(s["lv_h"], 2 * q + 1)
                A(hh[:, 4 + q], cg[:, q], ACT.Copy).then_inc(s["lv_h"], 1)
            for t in range(TT):
                act.wait_ge(s["m_u"], t + 1)
                A(hh[:, 0:GH, t * P:(t + 1) * P], mixed(t), ACT.Copy).then_inc(s["m_hi"], 1)
            for n in range(2):
                prep(U_OUT2 + n, n)
            for n in range(8):
                prep(U_OUT2 + n + 2, (n + 2) % 4)
                if n:
                    square(4, n - 1, X_OUT2)
            square(4, KT - 1, X_OUT2)
            norm_root(4)
            norm_halves(3)
            F = U_FFN2

            def relu_square(j, b):
                A(gc[:], acc(b), ACT.Relu).then_inc(s["r_relu"], 1)
                act.wait_ge(s["r_relu"], j + 1)
                act.wait_ge(s["a_lo"], FF1 + j)
                A(uc[:], gc[:], ACT.Square).then_inc(s["r_sq"], 1)
                act.wait_ge(s["r_sq"], j + 1)
                A(fh[:, b], uc[:], ACT.Copy).then_inc(s["a_hi"], 1)

            prep(F + 2, 2)
            act.wait_ge(s["w_used"], F + 1)
            relu_square(0, 0)
            with act.Fori(0, (FF2 - 2) // 2) as i:
                for u in range(2):
                    up = F + 1 + 2 * u
                    prep(up + 2, (3 + 2 * u) % 4, 4, i)
                    act.wait_ge(s["w_used"], up + 1 + 4 * i)
                    relu_square(2 * i + 1 + u, 1 - u)
                    prep(up + 3, (4 + 2 * u) % 4, 4, i)
            prep(U_END - 1, 3)
            act.wait_ge(s["w_used"], U_END - 2)
            relu_square(FF2 - 1, 1)
            norm_stats(5, X_FFN2 + KT * (FF2 - 1))
        @block.vector
        def _(dve):
            V_ = nc.vector
            TTo, STT, TS = V_.tensor_tensor, V_.scalar_tensor_tensor, V_.tensor_scalar
            chain = [0]

            def done(ins):
                chain[0] += 1
                ins.then_inc(s["v_chain"], 1)
                dve.wait_ge(s["v_chain"], chain[0])

            def prep(k, slot, m=0, i=0):
                dve.wait_ge(s["w_hi"], k + 1 + m * i)
                TTo(wls(slot), raw[:, k % 2], whs(slot).bitcast(F32), ALU.subtract).then_inc(s["w_lo"], 1)

            def add_square(r, k):
                if k < 1:
                    return
                dve.wait_ge(s["n_sq"], KT * r + k + 1)
                if k > 1:
                    dve.wait_ge(s["n_acc"], 7 * r + k - 1)
                TTo(nacc[:], nacc[:], sqt[:, k % 2], ALU.add).then_inc(s["n_acc"], 1)

            def norm_inverse(r):
                dve.wait_ge(s["n_cols"], r + 1)
                TS(small[:, 8:16], PS[:, 5, 0:8], 1.0 / D, EPS, ALU.mult, ALU.add).then_inc(s["n_v"], 1)
                dve.wait_ge(s["n_sd"], r + 1)
                done(V_.reciprocal(small[:, 24:32], small[:, 16:24]))

            def norm_factor(r):
                norm_inverse(r)
                TTo(diag[:], again(ident[:], TT), first(small[:, 24:32], P), ALU.mult).then_inc(s["n_diag"], 1)
                dve.wait_ge(s["n_R"], r + 1)

            def norm_halves(q, col):
                for k in range(KT + 1):
                    if k < KT:
                        if k >= 2:
                            dve.wait_ge(s["n_lo"], KT * q + k - 1)
                        STT(hf[:, k % 2], x[:, k], par[:, col + k:col + k + 1], acc(3), ALU.mult, ALU.mult).then_inc(s["n_x"], 1)
                    if k:
                        dve.wait_ge(s["n_hi"], KT * q + k)
                        TTo(hl[:, k - 1], hf[:, (k - 1) % 2], hh[:, k - 1].bitcast(F32), ALU.subtract).then_inc(s["n_lo"], 1)

            def norm_in_place(col, r=None):
                for k in range(KT):
                    STT(x[:, k], x[:, k], par[:, col + k:col + k + 1], acc(3), ALU.mult, ALU.mult).then_inc(s["x_written"], 1)
                    if r is not None:
                        add_square(r, k - 1)
                if r is not None:
                    add_square(r, KT - 1)

            dve.wait_ge(s["const_loaded"], 32)
            dve.wait_ge(s["par_mm"], 1)
            V_.tensor_copy(par[:, 0:109], PS[:, 4, 0:109]).then_inc(s["par_ready"], 1)
            V_.tensor_copy(par[:, 128:216], PS[:, 4, 128:216]).then_inc(s["par_ready"], 1)
            V_.tensor_copy(par[:, 256:300], PS[:, 4, 256:300]).then_inc(s["par_ready"], 1)
            V_.tensor_copy(par[:, 384:508], PS[:, 4, 384:508]).then_inc(s["par_ready"], 1)
            for k in range(KT):
                dve.wait_ge(s["xt_mm"], k + 1)
                V_.tensor_copy(x[:, k], acc(k % 2)).then_inc(s["x_written"], 1)
                add_square(0, k - 1)
            add_square(0, KT - 1)
            prep(0, 0)
            norm_factor(0)
            dve.wait_ge(s["par_ready"], 4)
            norm_halves(0, C_N1)
            prep(1, 1)
            dve.wait_ge(s["ba_hi"], 1)
            TTo(bal[:], baw[:], bah[:].bitcast(F32), ALU.subtract).then_inc(s["ba_lo"], 1)

            for n in range(12):
                prep(n + 2, (n + 2) % 4)
            with dve.Fori(0, 3) as i:
                for u in range(4):
                    prep(U_QKV + u + 2, (u + 2) % 4, 4, i)
                    dve.wait_ge(s["tap0"], 4 * i + u + 1)
                    for d in range(1, 4):
                        if d > 1:
                            dve.wait_ge(s["conv"], 12 * i + 3 * u + d - 1)
                        STT(cacc[:, u % 2, d:S], acc(u % 2)[:, 0:S - d],
                            par[:, bass.ds(C_CONV + 12 * (3 - d) + 4 * i + u, 1)], cacc[:, u % 2, d:S],
                            ALU.mult, ALU.add).then_inc(s["conv"], 1)
            prep(U_Z + 2, 2)
            dve.wait_ge(s["silu"], 12)
            dve.wait_ge(s["col_mm"], 12)
            dve.wait_ge(s["ba_mm"], 2)
            dve.wait_ge(s["rows_loaded"], 32)
            TS(tmpt[:, 0].rearrange("p (t c) -> p t c", c=8), PS[:, 7, 0:96].rearrange("p (t c) -> p t c", c=12)[:, :, 1:9],
               EPS, None, ALU.add).then_inc(s["tab_dve"], 1)
            ba = PS[:, 6, 0:64].rearrange("p (t c) -> p t c", c=8)
            done(TTo(tmpt[:, 4, 0:32].rearrange("p (t c) -> p t c", c=4), ba[:, :, 4:8], again(small[:, 0:4], TT), ALU.add))
            done(V_.tensor_copy(tmpt[:, 2, 0:32].rearrange("p (t c) -> p t c", c=4), ba[:, :, 0:4]))
            STT(tmpt[:, 4, 32:64], tmpt[:, 4, 0:32], -1.0, tmpt[:, 4, 0:32], ALU.mult, ALU.max).then_inc(s["tab_dve"], 1)
            dve.wait_ge(s["tab_act"], 4)
            done(V_.reciprocal(tmpt[:, 6], tmpt[:, 1]))
            rn = tmpt[:, 6].rearrange("p (t c) -> p t c", c=8)
            TS(tab[:, :, T_RQ:T_RQ + 4], rn[:, :, 0:4], float(P) ** -0.5, None, ALU.mult)
            V_.tensor_copy(tab[:, :, T_RK:T_RK + 4], rn[:, :, 4:8])
            V_.tensor_copy(tab[:, :, T_BETA:T_BETA + 4], tmpt[:, 3, 0:32].rearrange("p (t c) -> p t c", c=4))
            e, w, zz, z2, pl = tmpt[:, 5, 0:32], tmpt[:, 5, 32:64], tmpt[:, 7, 0:32], tmpt[:, 7, 32:64], tmpt[:, 3, 32:64]
            done(TS(w, e, 2.0, None, ALU.add))
            done(V_.reciprocal(w, w))
            done(TTo(zz, e, w, ALU.mult))
            done(TTo(z2, zz, zz, ALU.mult))
            done(TS(pl, z2, 1.0 / 17, None, ALU.mult))
            for n in (15, 13, 11, 9, 7, 5, 3):
                done(STT(pl, pl, 1.0 / n, z2, ALU.add, ALU.mult))
            done(STT(pl, pl, 1.0, zz, ALU.add, ALU.mult))
            done(TS(w, tmpt[:, 4, 0:32], 0.0, None, ALU.max))
            done(STT(pl, pl, 2.0, w, ALU.mult, ALU.add))
            done(STT(tab[:, :, T_G:T_G + 4], pl.rearrange("p (t c) -> p t c", c=4), -1.0,
                     again(small[:, 24:28], TT), ALU.mult, ALU.mult))
            dve.sem_inc(s["tab_dve"], 1)
            prep(U_Z + 3, 3)
            for n in range(2):
                prep(U_OUT1 + n, n)
            dve.wait_ge(s["tab_mm"], 1)
            done(TS(tab[:, :, T_NGC:T_NGC + 4], PS[:, 5, 0:32].rearrange("p (t c) -> p t c", c=4), -1.0, None, ALU.mult))
            end_phase(dve, 1)


            dve.sem_inc(s["s_max"], 1)
            dve.sem_inc(s["ob_ready"], 1)
            dve.sem_inc(s["obl_ready"], 1)

            def begin(c, p):
                V_.tensor_copy(cc[:, p], tab[:, bass.ds(c, 1), :].rearrange("p a n -> p (a n)")).then_inc(s["cc_ready"], 1)

            def load(c, p):
                dve.wait_ge(s["cc_ready"], c + 1)
                dve.wait_ge(s["gam_ready"], c + 1)
                TTo(G["E"][:], heads(0), first(cc[:, p, T_NGC:T_NGC + 4], P), ALU.add).then_inc(s["d_ready"], 1)
                dve.wait_ge(s["d_ready"], 2 * c + 1)
                TS(G["E"][:], G["E"][:], 0.0, None, ALU.min).then_inc(s["d_ready"], 1)

            def gram(c, p):
                dve.wait_ge(s["kq_mm"], 2 * c + 1)
                TTo(G["kn"][:], heads(1), first(cc[:, p, T_RK:T_RK + 4], P), ALU.mult).then_inc(s["kqn_ready"], 1)
                dve.wait_ge(s["kq_mm"], 2 * c + 2)
                TTo(G["qn"][:], heads(2), first(cc[:, p, T_RQ:T_RQ + 4], P), ALU.mult).then_inc(s["kqn_ready"], 1)

            def mix(c, p):
                dve.wait_ge(s["ot_mm"], c + 1)
                STT(G["og"][:], heads(7), par[:, C_GN:C_GN + 1], ch[:, p, 12:16], ALU.mult, ALU.mult)\
                    .then_inc(s["og_ready"], 1)

            def mix_low(c):
                dve.wait_ge(s["oh_ready"], c + 1)
                TTo(hl[:, 0:GH, bass.ds(c * P, P)], G["og"][:], hh[:, 0:GH, bass.ds(c * P, P)].bitcast(F32),
                    ALU.subtract).then_inc(s["ol_ready"], 1)

            begin(0, 0)
            load(0, 0)
            gram(0, 0)
            dve.wait_ge(s["tables_loaded"], 32)

            def turn(i, p, first_chunk, last):
                c = 2 * i + p
                g0 = 24 * i + 12 * p
                for stage in ORDER:
                    if stage == "turn_back":
                        dve.wait_ge(s["e_ready"], c + 1)
                        dve.wait_ge(s["tri_ready"], 2 * c + 2)
                        TTo(G["E"][:], G["E"][:], G["bm"][:], ALU.mult).then_inc(s["eb_ready"], 1)
                    elif stage == "pairs":
                        dve.wait_ge(s["gram_mm"], 2 * c + 1)
                        dve.wait_ge(s["eb_ready"], c + 1)
                        TTo(G["LT"][:], heads(1), G["E"][:], ALU.mult).then_inc(s["lat_ready"], 1)
                        dve.wait_ge(s["gram_mm"], 2 * c + 2)
                        TTo(G["AT"][:], heads(2), G["E"][:], ALU.mult).then_inc(s["lat_ready"], 1)
                    elif stage[0] == "corner":
                        l = stage[1]
                        dve.wait_ge(s["lev_l"], 6 * c + l)
                        TTo(G["U"][:], heads(0), again(lmask[:, 1 + l], GH), ALU.mult).then_inc(s["lev_u"], 1)
                    elif stage[0] == "join":
                        l = stage[1]
                        if l < 6:
                            dve.wait_ge(s["lev_v"], 5 * c + l)
                            TTo(G["T"][:], G["T"][:], heads(1), ALU.subtract).then_inc(s["lev_t"], 1)
                        dve.wait_ge(s["lev_w"], 6 * c + l)
                        TTo(G["TT"][:], G["TT"][:], heads(2), ALU.subtract).then_inc(s["lev_tt"], 1)
                    elif stage == "begin" and not last:
                        begin(c + 1, 1 - p)
                    elif stage == "read":
                        dve.wait_ge(s["ks_mm"], c + 1)
                        dve.wait_ge(s["v_ready"], c + 1)
                        TTo(G["v"][:], G["v"][:], heads(0), ALU.subtract).then_inc(s["r_ready"], 1)
                    elif stage == "update":
                        dve.wait_ge(s["os_mm"], 2 * c + 2)
                        dve.wait_ge(s["sg_ready"], c + 1)
                        TTo(G["St"][:], G["Sg"][:], heads(0), ALU.add).then_inc(s["s_ready"], 1)
                        dve.wait_ge(s["osq"], c + 1)
                        V_.tensor_reduce(oc[:, 0], G["v"][:], AX_X, ALU.add).then_inc(s["o_v"], 1)
                        dve.wait_ge(s["o_v"], 2 * c + 1)
                        TS(oc[:, 1], oc[:, 0], 1.0 / P, EPS, ALU.mult, ALU.add).then_inc(s["o_v"], 1)
                    elif stage == "load" and not last:
                        load(c + 1, 1 - p)
                    elif stage == "heads" and p == 1:
                        dve.wait_ge(s["obh_ready"], i + 1)
                        TTo(hl[:, bass.ds(4 + i, 1), :].rearrange("p a s -> p (a s)"),
                            PS[:, 3:5, :].rearrange("p a b -> p (a b)"),
                            hh[:, bass.ds(4 + i, 1), :].rearrange("p a s -> p (a s)").bitcast(F32),
                            ALU.subtract).then_inc(s["obl_ready"], 1)
                    elif stage == "gram" and not last:
                        gram(c + 1, 1 - p)
                    elif stage == "root":
                        dve.wait_ge(s["o_sd"], c + 1)
                        V_.reciprocal(oc[:, 3], oc[:, 2]).then_inc(s["o_r"], 1)
                    elif stage == "mix" and not first_chunk:
                        mix(c - 1, 1 - p)
                    elif stage == "invert":
                        dve.wait_ge(s["l_mm"], c + 1)
                        TTo(G["U"][:], heads(0), again(lmask[:, 1], GH), ALU.mult).then_inc(s["u0_ready"], 1)
                        dve.wait_ge(s["u0_ready"], c + 1)
                        TTo(G["T"][:], again(ident[:], GH), G["U"][:], ALU.subtract).then_inc(s["lev_t"], 1)
                        if not first_chunk:
                            mix_low(c - 1)
                    elif stage[0] == "scores" and stage[1] < 8:
                        h, n, k = stage[1], P * (stage[1] + 1), 8 * p + stage[1]
                        dve.wait_ge(s["s_mm"], 16 * i + k + 1)
                        if h >= 2:
                            dve.wait_ge(s["p_mm"], g0 + groups(h - 2)[-1][0] + 1)
                        V_.memset(small[:, 255:256], 0.0)
                        V_.tensor_tensor_reduce(out=sm[:, h % 2, 0:n],
                                                in0=PS[:, 3:5, :].rearrange("p a b -> p (a b)")[:, 0:n],
                                                in1=strip[:, S - n:S], scale=1.0, scalar=-3e38, op0=ALU.add,
                                                op1=ALU.max, accum_out=ac[:, 0, k:k + 1]).then_inc(s["s_max"], 1)
                        dve.wait_ge(s["s_max"], 16 * i + k + 2)
                        TS(ac[:, 1, k:k + 1], ac[:, 0, k:k + 1], -1.0, None, ALU.mult).then_inc(s["s_neg"], 1)
                    elif stage[0] == "weigh" and stage[1] >= 2:
                        h, k = stage[1] - 2, 8 * p + stage[1] - 2
                        dve.wait_ge(s["s_exp"], 16 * i + k + 1)
                        V_.reciprocal(ac[:, 3, k:k + 1], ac[:, 2, k:k + 1]).then_inc(s["rd_ready"], 1)
                        dve.wait_ge(s["rd_ready"], 16 * i + k + 1)
                        dve.wait_ge(s["pv_mm"], g0 + groups(h)[-1][0] + 3)
                        TS(ob[:, h, 64 * p:64 * p + 64], PS[:, 7, 0:64], ac[:, 3, k:k + 1], None, ALU.mult)\
                            .then_inc(s["ob_ready"], 1)

            turns(dve, turn)
            mix(TT - 1, 1)
            mix_low(TT - 1)
            end_phase(dve, 2)

            def residual(k, bank):
                TTo(x[:, k], x[:, k], acc(bank), ALU.add).then_inc(s["x_written"], 1)

            for n in range(8):
                prep(U_OUT1 + n + 2, (n + 2) % 4)
                dve.wait_ge(x_back[n // 4], 16)
                dve.wait_ge(s["w_used"], U_OUT1 + n + 1)
                residual(n, n % 2)
                add_square(1, n - 1)
            add_square(1, KT - 1)
            norm_factor(1)
            norm_halves(1, C_N2)

            F = U_FFN1

            def taps(dst, bank, col, tap0, conv, j):
                dve.wait_ge(s[tap0], j + 1)
                STT(dst[:, 1:S], acc(bank)[:, 0:S - 1], par[:, bass.ds(C_FF01 + 2 * FF1 + col, 1)], dst[:, 1:S],
                    ALU.mult, ALU.add).then_inc(s[conv], 1)
                dve.wait_ge(s[conv], 2 * j + 1)
                STT(dst[:, 2:S], acc(bank)[:, 0:S - 2], par[:, bass.ds(C_FF01 + col, 1)], dst[:, 2:S],
                    ALU.mult, ALU.add).then_inc(s[conv], 1)

            def inner(j, b):
                taps(uc, 1, j + FF1, "v_tap0", "v_conv", j)
                dve.wait_ge(s["v_conv"], 2 * j + 2)
                dve.wait_ge(s["f_silu"], j + 1)
                TTo(uc[:], gc[:], uc[:], ALU.mult).then_inc(s["a_f"], 1)
                low_a(j + 1, b)

            def low_a(count, b):
                dve.wait_ge(s["a_hi"], count)
                TTo(fl[:, b], uc[:], fh[:, b].bitcast(F32), ALU.subtract).then_inc(s["a_lo"], 1)

            def downs(j, m, i, unit, r=None):
                for t in range(KT):
                    if t < KT - 1:
                        dve.wait_ge(s["d_mm"], 7 * j + t + 1 + 7 * m * i)
                    else:
                        dve.wait_ge(s["w_used"], unit)
                    residual(t, 2 + t % 2)
                    if r is not None:
                        add_square(r, t - 1)
                if r is not None:
                    add_square(r, KT - 1)

            prep(F + 2, 2)
            taps(gc, 0, 0, "f_tap0", "f_conv", 0)
            prep(F + 3, 3)
            with dve.Fori(0, (FF1 - 2) // 2) as i:
                for u in range(2):
                    j = 2 * i + 1 + u
                    g = F + 2 + 3 * u
                    prep(g + 2, (g + 2 - F) % 6, 6, i)
                    inner(j - 1, u)
                    prep(g + 3, (g + 3 - F) % 6, 6, i)
                    taps(gc, 0, j, "f_tap0", "f_conv", j)
                    prep(g + 4, (g + 4 - F) % 6, 6, i)
                    downs(u, 2, i, g + 3 + 6 * i)
            g = U_IN2 - 4
            prep(g + 2, (g + 2 - F) % 6)
            inner(FF1 - 2, 0)
            prep(g + 3, (g + 3 - F) % 6)
            taps(gc, 0, FF1 - 1, "f_tap0", "f_conv", FF1 - 1)
            downs(FF1 - 2, 0, 0, g + 3)
            inner(FF1 - 1, 1)
            downs(FF1 - 1, 0, 0, g + 4, 2)
            prep(U_IN2, 0)
            norm_factor(2)
            norm_in_place(C_NF, 3)
            norm_factor(3)
            norm_halves(2, C_M1)
            prep(U_IN2 + 1, 1)

            V = U_IN2

            def gated(q):
                dve.wait_ge(s["g_sig"], q + 1)
                TTo(cg[:, q + 1], acc(2 * (q % 2)), sgb[:], ALU.mult).then_inc(s["g_ready"], 1)

            prep(V + 2, 2)
            prep(V + 3, 3)
            tap = 0
            for q in range(4):
                for d in range(TAPS31):
                    if tap % 21 == 0 and tap // 21 < 4:
                        gated(tap // 21)
                    if tap % 9 == 3 and tap // 9 < 12:
                        prep(V + 4 + tap // 9, (tap // 9) % 4)
                    w = tap31(q, d)
                    if d == 0:
                        dve.wait_ge(s["g_ready"], q + 1)
                        if q:
                            dve.wait_ge(s["p_chain"], TAPS31 * q)
                        done(TS(cg[:, q, CUT31:S], cg[:, q + 1, CUT31:S], w, par[:, C_CB + q:C_CB + q + 1],
                                ALU.mult, ALU.add))
                    else:
                        done(STT(cg[:, q, CUT31:S], cg[:, q + 1, CUT31 - d:S - d], w, cg[:, q, CUT31:S],
                                 ALU.mult, ALU.add))
                    tap += 1
                dve.sem_inc(s["c_dve"], 1)

            def centre(q):
                dve.wait_ge(s["lm_mm"], q + 1)
                STT(cg[:, q], acc(q % 2), -1.0 / P, cg[:, q], ALU.mult, ALU.add).then_inc(s["lm_x"], 1)

            def variance(q):
                dve.wait_ge(s["lv_mm"], q + 1)
                TS(small[:, 96 + 8 * q:104 + 8 * q], PS[:, 2 * (q % 2), 0:8], 1.0 / P, EPS, ALU.mult, ALU.add)\
                    .then_inc(s["lv_v"], 1)

            def diagonal(q):
                TTo(spread(q), again(ident[:], TT), first(small[:, 160 + 8 * q:168 + 8 * q], P), ALU.mult)\
                    .then_inc(s["lv_d"], 1)

            def scaled(q):
                dve.wait_ge(s["lv_R"], q + 1)
                TTo(cg[:, q], cg[:, q], acc(q % 2), ALU.mult).then_inc(s["lv_n"], 1)

            def value_gain(t):
                dve.wait_ge(s["v_ssq"], t + 1)
                STT(vt[:, t], vt[:, t], small[:, 40 + t:41 + t], lng[:], ALU.add, ALU.mult).then_inc(s["v_n1"], 1)

            dve.wait_ge(s["wt_mm"], 1)
            TTo(sgw[:, 1], heads(0), again(triu[:], GH), ALU.mult).then_inc(s["wt_ready"], 1)
            dve.wait_ge(s["sgu_loaded"], 64)
            for t in range(TT):
                dve.wait_ge(s["v_gelu"], t + 1)
                TS(small[:, 40 + t:41 + t], small[:, 32 + t:33 + t], -1.0 / HALF, None, ALU.mult).then_inc(s["v_neg"], 1)
                if t == LN0:
                    centre(0)
                    centre(1)
                if 0 <= t - LN0 - 1 < 4:
                    variance(t - LN0 - 1)
                if 2 <= t - LN0 <= 3:
                    centre(t - LN0)
                if t == LN0 + 4:
                    dve.wait_ge(s["lv_sd"], 1)
                    done(V_.reciprocal(small[:, 160:192], small[:, 128:160]))
                    diagonal(0)
                    diagonal(1)
                if t >= 2:
                    value_gain(t - 2)
            value_gain(TT - 2)
            value_gain(TT - 1)
            TS(small[:, 56:64], small[:, 48:56], 1.0 / HALF, EPS, ALU.mult, ALU.add).then_inc(s["v_var"], 1)
            scaled(0)
            scaled(1)
            dve.wait_ge(s["lv_R"], 2)
            diagonal(2)
            diagonal(3)
            dve.wait_ge(s["v_sd"], 1)
            done(V_.reciprocal(small[:, 72:80], small[:, 64:72]))
            dve.wait_ge(s["v_n1"], TT)
            for t in range(TT):
                STT(vt[:, t], vt[:, t], small[:, 72 + t:73 + t], lnb[:], ALU.mult, ALU.add).then_inc(s["v_n2"], 1)
            scaled(2)
            scaled(3)
            for t in range(TT + 1):
                if t < TT:
                    dve.wait_ge(s["m_mm"], TT + t + 1)
                    if t >= 2:
                        dve.wait_ge(s["m_lo"], t - 1)
                    TTo(mixed(t), PS[:, 4 + t % 4, :].rearrange("p (h t) -> p h t", h=GH), bsb[:], ALU.add)\
                        .then_inc(s["m_b"], 1)
                if t:
                    q = t - 1
                    dve.wait_ge(s["m_hi"], t)
                    TTo(hl[:, 0:GH, q * P:(q + 1) * P], mixed(q), hh[:, 0:GH, q * P:(q + 1) * P].bitcast(F32),
                        ALU.subtract).then_inc(s["m_lo"], 1)
                if t >= 5:
                    q = t - 5
                    dve.wait_ge(s["lv_h"], 2 * q + 2)
                    TTo(hl[:, 4 + q], cg[:, q], hh[:, 4 + q].bitcast(F32), ALU.subtract).then_inc(s["lv_l"], 1)

            prep(U_OUT2, 0)
            prep(U_OUT2 + 1, 1)
            for n in range(8):
                prep(U_OUT2 + n + 2, (n + 2) % 4)
                dve.wait_ge(s["w_used"], U_OUT2 + n + 1)
                residual(n, n % 2)
                add_square(4, n - 1)
            add_square(4, KT - 1)
            norm_factor(4)
            norm_halves(3, C_M2)

            F = U_FFN2
            prep(F + 2, 2)
            with dve.Fori(0, (FF2 - 2) // 2) as i:
                for u in range(2):
                    up = F + 1 + 2 * u
                    low_a(FF1 + 1 + u + 2 * i, u)
                    prep(up + 2, (3 + 2 * u) % 4, 4, i)
                    downs(FF1 + u, 2, i, up + 2 + 4 * i)
                    prep(up + 3, (4 + 2 * u) % 4, 4, i)
            low_a(FF1 + FF2 - 1, 0)
            prep(U_END - 1, 3)
            downs(FF1 + FF2 - 2, 0, 0, U_END - 1)
            low_a(FF1 + FF2, 1)
            downs(FF1 + FF2 - 1, 0, 0, U_END, 5)
            norm_inverse(5)
            dve.wait_ge(s["tables_loaded"], 48)
            for t in range(TT):
                dve.wait_ge(s["fin_mm"], t + 1)
                if t >= 4:
                    dve.wait_ge(out_stored[t % 4], 16 * (t // 4))
                STT(out_tile(t), out_acc(t), small[:, 24 + t:25 + t], raw[:, 0], ALU.mult, ALU.mult).then_inc(s["fin_evac"], 1)

        @block.tensor
        def _(pe):
            mm, tr = nc.tensor.matmul, nc.tensor.transpose

            def unit(k, slot, bank, m=0, i=0, stats=None):
                pe.wait_ge(s["w_lo"], k + 1 + m * i)
                for kk in range(KT):
                    if stats is not None:
                        pe.wait_ge(s["n_lo"], KT * stats + kk + 1)
                    cut = slice(kk * P, kk * P + P)
                    for n, (w, h) in enumerate(((whs, hh), (whs, hl), (wls, hh))):
                        for t in range(2):
                            last = mm(acc(bank)[:, t * HALF:(t + 1) * HALF], w(slot)[:, cut],
                                      h[:, kk, t * HALF:(t + 1) * HALF], start=kk == 0 and n == 0,
                                      stop=kk == KT - 1 and n == 2)
                last.then_inc(s["w_used"], 1)

            def down(k, slot, b, count, xw, m=0, i=0):
                pe.wait_ge(s["w_lo"], k + 1 + m * i)
                pe.wait_ge(s["a_lo"], count)
                for t in range(KT):
                    pe.wait_ge(s["x_written"], xw + t - 1)
                    cut = slice(t * P, t * P + P)
                    for n, (w, h) in enumerate(((whs, fh), (whs, fl), (wls, fh))):
                        for q in range(2):
                            last = mm(acc(2 + t % 2)[:, q * HALF:(q + 1) * HALF], w(slot)[:, cut],
                                      h[:, b, q * HALF:(q + 1) * HALF], start=n == 0, stop=n == 2)
                    last.then_inc(s["d_mm" if t < KT - 1 else "w_used"], 1)

            def columns(src, dst, stop):
                for t in range(TT):
                    last = mm(dst(t), src[:, t * P:(t + 1) * P], ones[:, 0:1], start=True, stop=True)
                last.then_inc(*stop)

            def norm_columns(r):
                pe.wait_ge(s["n_acc"], 7 * r + 7)
                columns(nacc, lambda t: PS[:, 5, t:t + 1], (s["n_cols"], 1))

            def norm_factor(r):
                norm_columns(r)
                pe.wait_ge(s["n_diag"], r + 1)
                for t in range(2):
                    last = mm(acc(3)[:, t * HALF:(t + 1) * HALF], ones[:], diag[:, 4 * t:4 * t + 4, :], start=True, stop=True)
                last.then_inc(s["n_R"], 1)

            def tokens(u, dst, free):
                pe.wait_ge(s["w_lo"], u + 4)
                for t in range(TT):
                    free(t)
                    for kk in range(KT):
                        cut = slice(kk * P, kk * P + P)
                        for n, (w, h) in enumerate(((wh, hh), (wl, hh), (wh, hl))):
                            last = mm(dst(t), h[:, kk, t * P:(t + 1) * P], w[:, :, cut], start=kk == 0 and n == 0,
                                      stop=kk == KT - 1 and n == 2)
                    yield last, t

            pe.wait_ge(s["const_loaded"], 32)
            pe.wait_ge(s["pack_loaded"], 16 * 14)
            for n, r in enumerate((109, 88, 44, 124)):
                last = tr(PS[:, 4, n * P:n * P + r], pack[0:r, n], ident[0:r, 0:r])
            last.then_inc(s["par_mm"], 1)
            pe.wait_ge(s["xin_loaded"], 16)
            for k in range(KT):
                if k >= 2:
                    pe.wait_ge(s["x_written"], k - 1)
                for t in range(TT):
                    last = tr(acc(k % 2)[:, t * P:(t + 1) * P], xin[:, t, k * P:(k + 1) * P], ident[:])
                last.then_inc(s["xt_mm"], 1)
            pe.wait_ge(s["consts_set"], 1)
            pe.wait_ge(s["x_written"], KT)
            pe.wait_ge(s["par_ready"], 4)
            norm_factor(0)
            for n in range(12):
                if n >= 2:
                    pe.wait_ge(s["st_written"], n - 1)
                unit(n, n % 4, n % 2, stats=0 if n == 0 else None)

            pe.wait_ge(s["sq_init"], 1)
            with pe.Fori(0, 3) as i:
                for u in range(4):
                    pe.wait_ge(s["st_written"], 11 + 4 * i + u)
                    unit(U_QKV + u, u, u % 2, 4, i)
                    pe.wait_ge(s["st_written"], 12 + 4 * i + u)
                    for tt in range(TT):
                        last = mm(PS[:, 7, bass.ds(tt * 12 + 4 * i + u, 1)], sqb[:, tt * P:(tt + 1) * P], ones[:, 0:1],
                                  start=True, stop=True)
                    last.then_inc(s["col_mm"], 1)

            pe.wait_ge(s["ba_lo"], 1)
            for kk in range(KT):
                for n, (w, h) in enumerate(((bah, hh), (bah, hl), (bal, hh))):
                    for q in range(2):
                        last = mm(PS[0:8, 4 + q, :], w[:, kk, :], h[:, kk, q * HALF:(q + 1) * HALF],
                                  start=kk == 0 and n == 0, stop=kk == KT - 1 and n == 2)
            last.then_inc(s["ba_mm"], 1)
            for n in range(4):
                pe.wait_ge(s["st_written"], U_Z + n - 1)
                unit(U_Z + n, n, n % 2)
                if n == 0:
                    pe.wait_ge(s["ba_copied"], 1)
                    for t in range(TT):
                        last = tr(PS[:, 6, 8 * t:8 * t + 8], cacc[0:8, 1, t * P:(t + 1) * P], ident[0:8, 0:8])
                    last.then_inc(s["ba_mm"], 1)
                elif n == 2:
                    pe.wait_ge(s["tab_dve"], 3)
                    mm(PS[:, 5, 0:32], triu[:], tab[:, :, T_G:T_G + 4], start=True, stop=True).then_inc(s["tab_mm"], 1)
            end_phase(pe, 1)

            def four(bank, left, right, start=True, stop=True):
                for h in range(GH):
                    last = mm(heads(bank)[:, h], left[:, h], right[:, h], start=start, stop=stop)
                return last

            def turn_tiles(bank, src):
                for h in range(GH):
                    last = tr(heads(bank)[:, h], src[:, h], ident[:])
                return last

            def load(c, p, turns_before):
                pe.wait_ge(ch_loaded[p], 16 * (turns_before + 1))
                turn_tiles(1, ch[:, p, 4:8]).then_inc(s["kq_mm"], 1)
                pe.wait_ge(s["tri_ready"], 2 * c + 1)
                pe.wait_ge(s["s_ready"], c + 1)
                mm(PS[:, 0, :], ones[:], G["U"][:], start=True, stop=True).then_inc(s["gc_mm"], 1)

            def gram(c, p):
                turn_tiles(2, ch[:, p, 0:4]).then_inc(s["kq_mm"], 1)
                pe.wait_ge(s["d_ready"], 2 * c + 1)
                pe.wait_ge(s["gam_ready"], c + 1)
                turn_tiles(0, ch[:, p, 8:12]).then_inc(s["v_mm"], 1)

            def mix(c):
                pe.wait_ge(s["on_ready"], c + 1)
                pe.wait_ge(s["ob_ready"], 8 * c + 9)
                turn_tiles(7, G["oz"]).then_inc(s["ot_mm"], 1)

            pe.sem_inc(s["pv_mm"], 2)
            load(0, 0, 0)
            gram(0, 0)

            def turn(i, p, first_chunk, last_chunk):
                c = 2 * i + p
                g0 = 24 * i + 12 * p
                for stage in ORDER:
                    if stage == "values" and p == 0:
                        pe.wait_ge(pair_loaded, 16 * (i + 1))
                        pe.wait_ge(s["obl_ready"], i + 1)
                        for t in range(TT):
                            last = tr(PS[:, 3 + t // 4, (t % 4) * P:(t % 4 + 1) * P], qkvb[:, 2, t * P:(t + 1) * P], ident[:])
                        last.then_inc(s["vt_mm"], 1)
                    elif stage == "turn_back":
                        pe.wait_ge(s["kqn_ready"], 2 * c + 2)
                        turn_tiles(1, G["kn"]).then_inc(s["kqT_mm"], 1)
                        turn_tiles(2, G["qn"]).then_inc(s["kqT_mm"], 1)
                    elif stage == "pairs":
                        pe.wait_ge(s["kqT_ready"], 2 * c + 1)
                        four(1, G["knT"], G["knT"]).then_inc(s["gram_mm"], 1)
                        pe.wait_ge(s["kqT_ready"], 2 * c + 2)
                        four(2, G["knT"], G["qnT"]).then_inc(s["gram_mm"], 1)
                    elif stage == "invert":
                        pe.wait_ge(s["lat_ready"], 2 * c + 1)
                        pe.wait_ge(s["v_ready"], c + 1)
                        turn_tiles(0, G["LT"]).then_inc(s["l_mm"], 1)
                    elif stage[0] == "corner":
                        pe.wait_ge(s["lev_t"], 6 * c + stage[1])
                        four(0, G["LT"], G["T"]).then_inc(s["lev_l"], 1)
                    elif stage[0] == "join":
                        l = stage[1]
                        pe.wait_ge(s["lev_u"], 6 * c + l)
                        if l == 1:
                            pe.wait_ge(s["tt0_ready"], 2 * c + 2)
                            pe.wait_ge(s["lat_ready"], 2 * c + 2)
                        else:
                            pe.wait_ge(s["lev_tt"], 6 * c + l - 1)
                        if l < 6:
                            four(1, G["TT"], G["U"]).then_inc(s["lev_v"], 1)
                        four(2, G["U"], G["TT"]).then_inc(s["lev_w"], 1)
                    elif stage == "read":
                        pe.wait_ge(s["kqd_ready"], 2 * c + 1)
                        four(0, G["kd"], G["St"]).then_inc(s["ks_mm"], 1)
                    elif stage == "solve":
                        pe.wait_ge(s["r_ready"], c + 1)
                        pe.wait_ge(s["lev_tt"], 6 * c + 6)
                        four(1, G["TT"], G["v"]).then_inc(s["u_mm"], 1)
                    elif stage == "update":
                        pe.wait_ge(s["kqd_ready"], 2 * c + 2)
                        pe.wait_ge(s["u_ready"], c + 1)
                        pe.wait_ge(s["ke_ready"], c + 1)
                        for h in range(GH):
                            mm(heads(2)[:, h], G["qd"][:, h], G["St"][:, h], start=True, stop=False)
                            last = mm(heads(2)[:, h], G["AT"][:, h], G["u"][:, h], start=False, stop=True)
                        last.then_inc(s["os_mm"], 1)
                        four(0, G["ke"], G["u"]).then_inc(s["os_mm"], 1)
                    elif stage == "load" and not last_chunk:
                        load(c + 1, 1 - p, i + p)
                    elif stage == "heads" and p == 1:
                        pe.wait_ge(s["ob_ready"], 16 * (i + 1) + 1)
                        for t in range(TT):
                            last = tr(PS[:, 3 + t // 4, (t % 4) * P:(t % 4 + 1) * P], ob[:, t], ident[:])
                        last.then_inc(s["obt_mm"], 1)
                    elif stage == "gram" and not last_chunk:
                        pe.wait_ge(s["o_copied"], c + 1)
                        gram(c + 1, 1 - p)
                    elif stage == "mix" and not first_chunk:
                        mix(c - 1)
                    elif stage[0] == "scores" and stage[1] < 8:
                        h, n = stage[1], P * (stage[1] + 1)
                        pe.wait_ge(s["s_max"], 16 * i + 8 * p + h + 1)
                        if p == 0 and h == 0:
                            pe.wait_ge(s["vb_ready"], i + 1)
                        rows_ = slice(64 * p, 64 * p + 64)
                        for lo in range(0, n, HALF):
                            hi = min(n, lo + HALF)
                            last = mm(PS[:, 3 + lo // HALF, 0:hi - lo], qkvb[rows_, 0, h * P:h * P + P],
                                      qkvb[rows_, 1, lo:hi], start=True, stop=True)
                        last.then_inc(s["s_mm"], 1)
                    elif stage[0] == "weigh":
                        if stage[1] <= 8:
                            h = stage[1] - 1
                            pe.wait_ge(s["s_exp"], 16 * i + 8 * p + h + 1)
                            for g, n in groups(h):
                                pe.wait_ge(s["p_evac"], g0 + g + 1)
                                b0 = 4 * (g - groups(h)[0][0])
                                for b in range(n):
                                    last = tr(PS[:, 5 + g % 2, b * P:b * P + P],
                                              sm[:, h % 2, (b0 + b) * P:(b0 + b) * P + P], ident[:])
                                last.then_inc(s["p_mm"], 1)
                        if stage[1] >= 2:
                            h = stage[1] - 2
                            pe.wait_ge(s["ob_ready"], 16 * i + 8 * p + h + 1)
                            if h == 0 and not first_chunk:
                                pe.wait_ge(s["og_ready"], c)
                            for g, n in groups(h):
                                pe.wait_ge(s["p_evac"], g0 + g + 3)
                                b0 = 4 * (g - groups(h)[0][0])
                                for b in range(n):
                                    last = mm(PS[:, 7, 0:64], pt[:, g % 2, b * P:b * P + P],
                                              vb[:, b0 + b, 64 * p:64 * p + 64], start=b0 + b == 0, stop=b0 + b == h)
                                last.then_inc(s["pv_mm"], 1)

            turns(pe, turn)
            mix(TT - 1)
            end_phase(pe, 2)

            for n in range(8):
                if n >= 2:
                    pe.wait_ge(s["x_written"], X_OUT1 + n - 1)
                unit(U_OUT1 + n, n % 4, n % 2)
            norm_factor(1)

            F = U_FFN1
            unit(F, 0, 0, stats=1)
            unit(F + 1, 1, 1)
            with pe.Fori(0, (FF1 - 2) // 2) as i:
                for u in range(2):
                    j = 2 * i + 1 + u
                    g = F + 2 + 3 * u
                    pe.wait_ge(s["f_conv"], 2 * j)
                    unit(g, (g - F) % 6, 0, 6, i)
                    pe.wait_ge(s["v_conv"], 2 * j)
                    unit(g + 1, (g + 1 - F) % 6, 1, 6, i)
                    down(g + 2, (g + 2 - F) % 6, u, j, X_FFN1 + KT * (j - 1), 6, i)
            g, j = U_IN2 - 4, FF1 - 1
            pe.wait_ge(s["f_conv"], 2 * j)
            unit(g, (g - F) % 6, 0)
            pe.wait_ge(s["v_conv"], 2 * j)
            unit(g + 1, (g + 1 - F) % 6, 1)
            down(g + 2, (g + 2 - F) % 6, 0, j, X_FFN1 + KT * (j - 1))
            down(g + 3, (g + 3 - F) % 6, 1, j + 1, X_FFN1 + KT * j)
            norm_factor(2)
            norm_factor(3)

            V = U_IN2
            for n in range(8):
                if n >= 4:
                    pe.wait_ge(s["g_ready"], n // 2 - 1)
                unit(V + n, n % 4, n % 4, stats=2 if n == 0 else None)
            for h in range(GH):
                if h < 2:
                    pe.wait_ge(s["g_ready"], 3)
                else:
                    pe.wait_ge(s["u_gelu"], h - 1)
                unit(V + 8 + h, h % 4, h % 2)

            def v_free(t):
                pe.wait_ge(s["g_ready"], 4)
                if t >= 4:
                    pe.wait_ge(s["v_ssq"], t - 3)

            def group_sums(q):
                pe.wait_ge(s["c_dve"], 4)
                pe.wait_ge(s["p_chain"], 4 * TAPS31)
                if q >= 2:
                    pe.wait_ge(s["lv_v"], q - 1)
                for t in range(2):
                    last = mm(acc(q % 2)[:, t * HALF:(t + 1) * HALF], ones[:], cg[:, q, t * HALF:(t + 1) * HALF],
                              start=True, stop=True)
                last.then_inc(s["lm_mm"], 1)

            def group_columns(q):
                pe.wait_ge(s["lm_sq"], q + 1)
                columns(sgb, lambda t: PS[:, 2 * (q % 2), t:t + 1], (s["lv_mm"], 1))

            def group_spread(q):
                pe.wait_ge(s["lv_d"], q + 1)
                if q >= 2:
                    pe.wait_ge(s["lv_n"], q - 1)
                for t in range(2):
                    last = mm(acc(q % 2)[:, t * HALF:(t + 1) * HALF], ones[:], spread(q)[:, 4 * t:4 * t + 4, :],
                              start=True, stop=True)
                last.then_inc(s["lv_R"], 1)

            for last, t in tokens(V + 12, lambda t: PS[:, 4 + t % 4, :], v_free):
                last.then_inc(s["m_mm"], 1)
                if t == 0:
                    pe.wait_ge(s["sgu_loaded"], 64)
                    pe.wait_ge(s["u_gelu"], GH)
                    turn_tiles(0, sgw[:, 0]).then_inc(s["wt_mm"], 1)
                elif t == LN0:
                    pe.wait_ge(s["wt_ready"], 1)
                    group_sums(0)
                    group_sums(1)
                elif 0 <= t - LN0 - 1 < 4:
                    group_columns(t - LN0 - 1)
                    if 2 <= t - LN0 <= 3:
                        group_sums(t - LN0)
            pe.drain().then_inc(s["w_used"], 4)
            for q in range(4):
                group_spread(q)
            for t in range(TT):
                pe.wait_ge(s["v_n2"], t + 1)
                if t >= 4:
                    pe.wait_ge(s["m_b"], t - 3)
                for h in range(GH):
                    last = mm(PS[:, 4 + t % 4, h * P:(h + 1) * P], vt[:, t, h * P:(h + 1) * P], sgw[:, 1, h],
                              start=True, stop=True)
                last.then_inc(s["m_mm"], 1)
            pe.wait_ge(s["lv_n"], 4)
            pe.wait_ge(s["m_lo"], TT)
            pe.wait_ge(s["lv_l"], 4)
            for n in range(8):
                if n >= 2:
                    pe.wait_ge(s["x_written"], X_OUT2 + n - 1)
                unit(U_OUT2 + n, n % 4, n % 2)
            norm_factor(4)

            F = U_FFN2
            unit(F, 0, 0, stats=3)
            with pe.Fori(0, (FF2 - 2) // 2) as i:
                for u in range(2):
                    j = 2 * i + 1 + u
                    up = F + 1 + 2 * u
                    pe.wait_ge(s["r_relu"], j)
                    unit(up, (1 + 2 * u) % 4, 1 - u, 4, i)
                    down(up + 1, (2 + 2 * u) % 4, u, FF1 + j, X_FFN2 + KT * (j - 1), 4, i)
            pe.wait_ge(s["r_relu"], FF2 - 1)
            unit(U_END - 3, 1, 1)
            down(U_END - 2, 2, 0, FF1 + FF2 - 1, X_END - 2 * KT)
            down(U_END - 1, 3, 1, FF1 + FF2, X_END - KT)
            pe.wait_ge(s["x_written"], X_END)
            for t in range(TT):
                if t == 2:
                    norm_columns(5)
                if t >= 3:
                    pe.wait_ge(s["fin_evac"], t - 2)
                for k in range(KT):
                    last = tr(out_acc(t)[:, k * P:(k + 1) * P], x[:, k, t * P:(t + 1) * P], ident[:])
                last.then_inc(s["fin_mm"], 1)


def groups(h):
    if h < 4:
        return [(h, h + 1)]
    return [(2 * h - 4, 4), (2 * h - 3, h - 3)]


def shape_constants():
    at = np.arange(P)
    levels = [((at[:, None] // b) % 2 == 1) & (at[None, :] // b == at[:, None] // b - 1) for b in (1 << l for l in range(LEVELS))]
    dist = at[:, None] + (S - P) - np.arange(S)[None, :]
    held = sum(((dist >= 0) & (dist <= window) & (dist % step == 0)).astype(int) for window, step in ((128, 1), (512, 4), (2048, 16)))
    return {"c_ident": np.eye(P, dtype=np.float32),
            "c_triu": (at[:, None] <= at[None, :]).astype(np.float32),
            "c_levels": np.stack([levels[0].T] + levels, 1).astype(np.float32),
            "c_strip": np.where(held > 0, np.log(np.maximum(held, 1)), -1e30).astype(np.float32)}


def kernel(**inputs):
    import concourse.bacc as bacc
    from concourse.bass_utils import run_bass_kernel_spmd

    arrays = {name: np.ascontiguousarray(value) for name, value in {**inputs, **shape_constants()}.items()}
    nc = bacc.Bacc("TRN2", target_bir_lowering=False, num_devices=1)
    a = {name: nc.dram_tensor("in_" + name, v.shape, F32, kind="ExternalInput").ap() for name, v in arrays.items()}
    out = nc.dram_tensor("out", (1, S, D), F32, kind="ExternalOutput").ap()
    program(nc, a, out)
    r = run_bass_kernel_spmd(nc, [{"in_" + name: v for name, v in arrays.items()}], core_ids=[0])
    return r.results[0]["out"]
```
